# Optimizing a Trainium2 kernel written in Bass

```python
import math
import jax, jax.numpy as jnp
from jax import lax
import numpy as np

D_MODEL = 1024
BATCH = 1
SEQ = 256
DEPTH = 1

CHUNK = 64
GMLP_BLOCK = 128
GMLP_GROUPS = 4
GMLP_WIDTH = D_MODEL
GMLP_GROUP_DIM = GMLP_WIDTH // GMLP_GROUPS
SB_HEADS = 16
SB_HEAD_DIM = 64
SB_WIDTH = SB_HEADS * SB_HEAD_DIM
SB_QBLOCK = 128
D_FF = 2816
N_BRANCHES = 2
D_IN = 2 * GMLP_WIDTH + 3 * SB_WIDTH + N_BRANCHES * D_MODEL
EPS = 1e-6


def rmsnorm(x, g):
    xf = x.astype(jnp.float32)
    y = xf * lax.rsqrt(jnp.mean(xf * xf, axis=-1, keepdims=True) + EPS)
    return (y * g.astype(jnp.float32)).astype(x.dtype)

def layernorm(x, g, b):
    xf = x.astype(jnp.float32)
    mu = jnp.mean(xf, axis=-1, keepdims=True)
    var = jnp.mean(jnp.square(xf - mu), axis=-1, keepdims=True)
    y = (xf - mu) * lax.rsqrt(var + EPS)
    return (y * g.astype(jnp.float32) + b.astype(jnp.float32)).astype(x.dtype)

def swiglu(x, w_gate, w_up, w_down):
    return (jax.nn.silu(x @ w_gate) * (x @ w_up)) @ w_down

def gmlp_spatial_gating(a, ln_g, ln_b, w_s, b_s):
    bsz, seq, _ = a.shape
    nblk = seq // GMLP_BLOCK
    u, v = jnp.split(a, 2, axis=-1)
    u = u.reshape(bsz, nblk, GMLP_BLOCK, GMLP_GROUPS, GMLP_GROUP_DIM)
    v = v.reshape(bsz, nblk, GMLP_BLOCK, GMLP_GROUPS, GMLP_GROUP_DIM)
    v = layernorm(v, ln_g, ln_b)
    pos = jnp.arange(GMLP_BLOCK)
    mask = (pos[None, :] // CHUNK) <= (pos[:, None] // CHUNK)
    w_masked = jnp.where(mask[None], w_s, jnp.zeros((), w_s.dtype))
    s_mix = jnp.einsum('gts,bnsgc->bntgc', w_masked, v) + jnp.transpose(b_s)[None, None, :, :, None]
    return (u * s_mix).reshape(bsz, seq, GMLP_WIDTH)

def stick_breaking_attention(q, k, v):
    q = jnp.transpose(q, (0, 2, 1, 3))
    k = jnp.transpose(k, (0, 2, 1, 3))
    v = jnp.transpose(v, (0, 2, 1, 3))
    seq = q.shape[2]
    scale = 1.0 / math.sqrt(SB_HEAD_DIM)
    outs = []
    for blk in range(seq // SB_QBLOCK):
        q0 = blk * SB_QBLOCK
        kend = q0 + SB_QBLOCK
        qb = q[:, :, q0:kend]
        kb = k[:, :, :kend]
        vb = v[:, :, :kend]
        z = jnp.einsum('bhtd,bhsd->bhts', qb, kb).astype(jnp.float32) * scale
        t_idx = q0 + jnp.arange(SB_QBLOCK)[:, None]
        s_idx = jnp.arange(kend)[None, :]
        causal = s_idx < t_idx
        log_keep = jnp.where(causal, -jax.nn.softplus(z), 0.0)
        log_w = jax.nn.log_sigmoid(z) + lax.cumsum(log_keep, axis=3, reverse=True) - log_keep
        w = jnp.where(causal, jnp.exp(log_w), 0.0)
        outs.append(jnp.einsum('bhts,bhsd->bhtd', w.astype(vb.dtype), vb))
    o = jnp.concatenate(outs, axis=2)
    return jnp.transpose(o, (0, 2, 1, 3))

def first_inputs(seed: int = 0) -> dict:
    key = jax.random.key(seed)
    ks = jax.random.split(key, 24)
    f32 = jnp.float32

    def nrm(k, shape, fan_in):
        return jax.random.normal(k, shape, f32) * (fan_in ** -0.5)

    def gain(k, shape):
        return 1.0 + 0.05 * jax.random.normal(k, shape, f32)

    L = DEPTH
    return {
        "x": jax.random.normal(ks[0], (BATCH, SEQ, D_MODEL), f32),
        "ff1_norm": gain(ks[1], (L, D_MODEL)),
        "ff1_w_gate": nrm(ks[2], (L, D_MODEL, D_FF), D_MODEL),
        "ff1_w_up": nrm(ks[3], (L, D_MODEL, D_FF), D_MODEL),
        "ff1_w_down": nrm(ks[4], (L, D_FF, D_MODEL), D_FF),
        "mix_norm": gain(ks[5], (L, D_MODEL)),
        "w_in": nrm(ks[6], (L, D_MODEL, D_IN), D_MODEL),
        "b_gate": 0.05 * jax.random.normal(ks[7], (L, N_BRANCHES * D_MODEL), f32),
        "gmlp_ln_g": gain(ks[8], (L, GMLP_GROUPS, GMLP_GROUP_DIM)),
        "gmlp_ln_b": 0.05 * jax.random.normal(ks[9], (L, GMLP_GROUPS, GMLP_GROUP_DIM), f32),
        "gmlp_w_s": nrm(ks[10], (L, GMLP_GROUPS, GMLP_BLOCK, GMLP_BLOCK), GMLP_BLOCK),
        "gmlp_b_s": 1.0 + 0.1 * jax.random.normal(ks[11], (L, GMLP_GROUPS, GMLP_BLOCK), f32),
        "w_branch_a": nrm(ks[12], (L, GMLP_WIDTH, D_MODEL), GMLP_WIDTH),
        "w_branch_b": nrm(ks[13], (L, SB_WIDTH, D_MODEL), SB_WIDTH),
        "w_out": nrm(ks[14], (L, D_MODEL, D_MODEL), D_MODEL),
        "ff2_norm": gain(ks[15], (L, D_MODEL)),
        "ff2_w_gate": nrm(ks[16], (L, D_MODEL, D_FF), D_MODEL),
        "ff2_w_up": nrm(ks[17], (L, D_MODEL, D_FF), D_MODEL),
        "ff2_w_down": nrm(ks[18], (L, D_FF, D_MODEL), D_FF),
        "final_norm": gain(ks[19], (D_MODEL,)),
    }

def first_block(x, ff1_norm, ff1_w_gate, ff1_w_up, ff1_w_down, mix_norm, w_in, b_gate,
              gmlp_ln_g, gmlp_ln_b, gmlp_w_s, gmlp_b_s, w_branch_a, w_branch_b, w_out,
              ff2_norm, ff2_w_gate, ff2_w_up, ff2_w_down, final_norm):
    bsz, seq, _ = x.shape
    splits = [2 * GMLP_WIDTH, 2 * GMLP_WIDTH + SB_WIDTH, 2 * GMLP_WIDTH + 2 * SB_WIDTH,
              2 * GMLP_WIDTH + 3 * SB_WIDTH]
    for l in range(DEPTH):
        x = x + 0.5 * swiglu(rmsnorm(x, ff1_norm[l]), ff1_w_gate[l], ff1_w_up[l], ff1_w_down[l])

        h = rmsnorm(x, mix_norm[l])
        proj = h @ w_in[l]
        a_in, q, k, v, g_logits = jnp.split(proj, splits, axis=-1)
        y_a = gmlp_spatial_gating(jax.nn.gelu(a_in, approximate=False),
                                  gmlp_ln_g[l], gmlp_ln_b[l], gmlp_w_s[l], gmlp_b_s[l])
        q = q.reshape(bsz, seq, SB_HEADS, SB_HEAD_DIM)
        k = k.reshape(bsz, seq, SB_HEADS, SB_HEAD_DIM)
        v = v.reshape(bsz, seq, SB_HEADS, SB_HEAD_DIM)
        y_b = stick_breaking_attention(q, k, v).reshape(bsz, seq, SB_WIDTH)
        gates = jax.nn.sigmoid(g_logits + b_gate[l])
        g_a, g_b = jnp.split(gates, 2, axis=-1)
        merged = g_a * (y_a @ w_branch_a[l]) + g_b * (y_b @ w_branch_b[l])
        x = x + merged @ w_out[l]

        x = x + 0.5 * swiglu(rmsnorm(x, ff2_norm[l]), ff2_w_gate[l], ff2_w_up[l], ff2_w_down[l])
    return rmsnorm(x, final_norm)


DEPTH_2 = 2

N_HEADS = 16
HEAD_DIM = D_MODEL // N_HEADS
D_FF_2 = 4 * D_MODEL
N_A_LAYERS = DEPTH_2 // 2
N_B_LAYERS = DEPTH_2 - N_A_LAYERS
MOBA_BLOCK = 256
MOBA_TOPK = 3
MOBA_Q_CHUNK = 16
FOX_Q_BLOCK = 128
RMS_EPS = 1e-6
NEG_INF = -1e30


def rms_norm(x, g):
    xf = x.astype(jnp.float32)
    y = xf * lax.rsqrt(jnp.mean(xf * xf, axis=-1, keepdims=True) + RMS_EPS)
    return (y * g.astype(jnp.float32)).astype(x.dtype)

def alibi_slopes(n):
    return jnp.asarray(2.0 ** (-8.0 * np.arange(1, n + 1) / n), dtype=jnp.float32)

def split_heads(t):
    b, s, _ = t.shape
    return t.reshape(b, s, N_HEADS, HEAD_DIM).transpose(0, 2, 1, 3)

def merge_heads(t):
    b, h, s, d = t.shape
    return t.transpose(0, 2, 1, 3).reshape(b, s, h * d)

def squared_relu_mlp(x, w_up, w_down):
    return jnp.square(jax.nn.relu(x @ w_up)) @ w_down

def moba_attention(q, k, v):
    b, h, s, d = q.shape
    nb = -(-s // MOBA_BLOCK)
    pad = ((0, 0), (0, 0), (0, nb * MOBA_BLOCK - s), (0, 0))
    kb = jnp.pad(k, pad).reshape(b, h, nb, MOBA_BLOCK, d)
    vb = jnp.pad(v, pad).reshape(b, h, nb, MOBA_BLOCK, d)
    scale = 1.0 / math.sqrt(d)
    slopes = alibi_slopes(h)[None, :, None, None]
    n_sel = min(MOBA_TOPK, nb - 1)
    own_blk = jnp.arange(s) // MOBA_BLOCK
    bi = jnp.arange(b)[:, None, None, None]
    hi = jnp.arange(h)[None, :, None, None]

    if n_sel > 0:
        k_mean = jnp.mean(kb.astype(jnp.float32), axis=3)
        gate = jnp.einsum('bhsd,bhnd->bhsn', q.astype(jnp.float32), k_mean)
        past = jnp.arange(nb)[None, :] < own_blk[:, None]
        gate = jnp.where(past, gate, NEG_INF)
        _, sel = lax.top_k(gate, n_sel)
        sel_valid = jnp.arange(n_sel)[None, :] < own_blk[:, None]

    n_chunks = s // MOBA_Q_CHUNK
    blk_offs = jnp.arange(MOBA_BLOCK)

    def chunk(ci):
        t0 = ci * MOBA_Q_CHUNK
        qc = lax.dynamic_slice_in_dim(q, t0, MOBA_Q_CHUNK, axis=2)
        tq = t0 + jnp.arange(MOBA_Q_CHUNK)
        blk = t0 // MOBA_BLOCK
        k_own = lax.dynamic_index_in_dim(kb, blk, axis=2, keepdims=False)
        v_own = lax.dynamic_index_in_dim(vb, blk, axis=2, keepdims=False)
        ks_own = blk * MOBA_BLOCK + blk_offs
        dist_own = (tq[:, None] - ks_own[None, :]).astype(jnp.float32)
        s_own = (jnp.einsum('bhcd,bhkd->bhck', qc, k_own).astype(jnp.float32) * scale
                 - slopes * dist_own)
        s_own = jnp.where(dist_own >= 0, s_own, NEG_INF)
        if n_sel > 0:
            sel_c = lax.dynamic_slice_in_dim(sel, t0, MOBA_Q_CHUNK, axis=2)
            valid_c = lax.dynamic_slice_in_dim(sel_valid, t0, MOBA_Q_CHUNK, axis=0)
            k_sel = kb[bi, hi, sel_c]
            v_sel = vb[bi, hi, sel_c]
            ks_sel = sel_c[..., None] * MOBA_BLOCK + blk_offs
            dist_sel = (tq[:, None, None] - ks_sel).astype(jnp.float32)
            s_sel = (jnp.einsum('bhcd,bhcnkd->bhcnk', qc, k_sel).astype(jnp.float32) * scale
                     - slopes[..., None] * dist_sel)
            s_sel = jnp.where(valid_c[:, :, None], s_sel, NEG_INF)
            scores = jnp.concatenate(
                [s_sel.reshape(b, h, MOBA_Q_CHUNK, n_sel * MOBA_BLOCK), s_own], axis=-1)
            p = jax.nn.softmax(scores, axis=-1)
            p_sel = p[..., :n_sel * MOBA_BLOCK].reshape(b, h, MOBA_Q_CHUNK, n_sel, MOBA_BLOCK).astype(v.dtype)
            p_own = p[..., n_sel * MOBA_BLOCK:].astype(v.dtype)
            return (jnp.einsum('bhcnk,bhcnkd->bhcd', p_sel, v_sel)
                    + jnp.einsum('bhck,bhkd->bhcd', p_own, v_own))
        p_own = jax.nn.softmax(s_own, axis=-1).astype(v.dtype)
        return jnp.einsum('bhck,bhkd->bhcd', p_own, v_own)

    outs = lax.map(chunk, jnp.arange(n_chunks))
    return outs.transpose(1, 2, 0, 3, 4).reshape(b, h, s, d)

def shared_kv(h, kv_norm, w_kv, w_f, b_f):
    hn = rms_norm(h, kv_norm)
    k, v = jnp.split(hn @ w_kv, 2, axis=-1)
    log_f = jax.nn.log_sigmoid((hn @ w_f + b_f).astype(jnp.float32))
    c = jnp.cumsum(log_f, axis=1).transpose(0, 2, 1)
    return split_heads(k), split_heads(v), c

def forgetting_attention(q, k, v, c):
    b, h, s, d = q.shape
    scale = 1.0 / math.sqrt(d)
    kpos = jnp.arange(s)

    def block(qi):
        t0 = qi * FOX_Q_BLOCK
        qb = lax.dynamic_slice_in_dim(q, t0, FOX_Q_BLOCK, axis=2)
        cq = lax.dynamic_slice_in_dim(c, t0, FOX_Q_BLOCK, axis=2)
        tq = t0 + jnp.arange(FOX_Q_BLOCK)
        sc = (jnp.einsum('bhqd,bhkd->bhqk', qb, k).astype(jnp.float32) * scale
              + cq[..., None] - c[:, :, None, :])
        sc = jnp.where(kpos[None, :] <= tq[:, None], sc, NEG_INF)
        p = jax.nn.softmax(sc, axis=-1).astype(v.dtype)
        return jnp.einsum('bhqk,bhkd->bhqd', p, v)

    outs = lax.map(block, jnp.arange(s // FOX_Q_BLOCK))
    return outs.transpose(1, 2, 0, 3, 4).reshape(b, h, s, d)

def second_inputs(seed: int = 0) -> dict:
    key = jax.random.key(seed)
    ks = jax.random.split(key, 14)
    D, F, H = D_MODEL, D_FF_2, N_HEADS
    nrm = lambda k, shape, fan_in, gain=1.0: (gain * fan_in ** -0.5) * jax.random.normal(k, shape, jnp.float32)
    return {
        "x": jax.random.normal(ks[0], (BATCH, SEQ, D), jnp.float32),
        "attn_norm": 1.0 + 0.02 * jax.random.normal(ks[1], (DEPTH_2, D), jnp.float32),
        "moba_w_qkv": nrm(ks[2], (N_A_LAYERS, D, 3 * D), D),
        "fox_w_q": nrm(ks[3], (N_B_LAYERS, D, D), D),
        "w_o": nrm(ks[4], (DEPTH_2, D, D), D, 0.5),
        "kv_norm": 1.0 + 0.02 * jax.random.normal(ks[5], (D,), jnp.float32),
        "w_kv": nrm(ks[6], (D, 2 * D), D),
        "w_f": nrm(ks[7], (D, H), D),
        "b_f": 3.0 + 0.5 * jax.random.normal(ks[8], (H,), jnp.float32),
        "mlp_norm": 1.0 + 0.02 * jax.random.normal(ks[9], (DEPTH_2, D), jnp.float32),
        "w_up": nrm(ks[10], (DEPTH_2, D, F), D),
        "w_down": nrm(ks[11], (DEPTH_2, F, D), F, 0.5),
        "final_norm": 1.0 + 0.02 * jax.random.normal(ks[12], (D,), jnp.float32),
    }

def second_block(x, attn_norm, moba_w_qkv, fox_w_q, w_o, kv_norm, w_kv, w_f, b_f,
              mlp_norm, w_up, w_down, final_norm):
    h = x
    k_sh = v_sh = c_sh = None
    for layer in range(DEPTH_2):
        if layer == N_A_LAYERS:
            k_sh, v_sh, c_sh = shared_kv(h, kv_norm, w_kv, w_f, b_f)
        hn = rms_norm(h, attn_norm[layer])
        if layer < N_A_LAYERS:
            q, k, v = jnp.split(hn @ moba_w_qkv[layer], 3, axis=-1)
            mix = moba_attention(split_heads(q), split_heads(k), split_heads(v))
        else:
            q = split_heads(hn @ fox_w_q[layer - N_A_LAYERS])
            mix = forgetting_attention(q, k_sh, v_sh, c_sh)
        h = h + merge_heads(mix) @ w_o[layer]
        h = h + squared_relu_mlp(rms_norm(h, mlp_norm[layer]), w_up[layer], w_down[layer])
    return rms_norm(h, final_norm)


def setup_inputs(seed=0):
    out = dict(first_inputs(seed))
    for name, value in second_inputs(seed + 1).items():
        if name != "x":
            out[name + "_2"] = value
    return out


def reference(
    x, ff1_norm, ff1_w_gate, ff1_w_up, ff1_w_down, mix_norm, w_in, b_gate, gmlp_ln_g, gmlp_ln_b,
    gmlp_w_s, gmlp_b_s, w_branch_a, w_branch_b, w_out, ff2_norm, ff2_w_gate, ff2_w_up,
    ff2_w_down, final_norm, attn_norm_2, moba_w_qkv_2, fox_w_q_2, w_o_2, kv_norm_2, w_kv_2,
    w_f_2, b_f_2, mlp_norm_2, w_up_2, w_down_2, final_norm_2,
):
    x = first_block(
        x, ff1_norm, ff1_w_gate, ff1_w_up, ff1_w_down, mix_norm, w_in, b_gate, gmlp_ln_g,
        gmlp_ln_b, gmlp_w_s, gmlp_b_s, w_branch_a, w_branch_b, w_out, ff2_norm, ff2_w_gate,
        ff2_w_up, ff2_w_down, final_norm,
    )
    return second_block(
        x, attn_norm_2, moba_w_qkv_2, fox_w_q_2, w_o_2, kv_norm_2, w_kv_2, w_f_2, b_f_2,
        mlp_norm_2, w_up_2, w_down_2, final_norm_2,
    )


_drawn_inputs = setup_inputs


def setup_inputs(seed=0):
    import zlib

    import numpy as np

    out = dict(_drawn_inputs(seed))
    spreads = {}
    factors = {'b_gate': 5.164,
     'gmlp_ln_g': 4.17,
     'gmlp_ln_b': 3.738,
     'ff2_norm': 2.975,
     'attn_norm_2': 8.0,
     'kv_norm_2': 8.0,
     'mlp_norm_2': 3.553,
     'final_norm_2': 2.854}
    for name, (base, spread) in spreads.items():
        noise = np.random.default_rng([zlib.crc32(name.encode()), seed]).standard_normal(out[name].shape)
        drawn = base * np.exp(spread * noise) if base else spread * noise
        out[name] = __import__('jax').numpy.asarray(drawn.astype(out[name].dtype))
    for name, factor in factors.items():
        out[name] = (out[name] * factor).astype(out[name].dtype)
    return out
```

```python
from contextlib import ExitStack

import numpy as np
import concourse.bass as bass
from concourse import mybir
from concourse.alu_op_type import AluOpType as ALU

ACT = mybir.ActivationFunctionType
F32 = mybir.dt.float32
F32R = mybir.dt.float32r
BF16 = mybir.dt.bfloat16
I32 = mybir.dt.int32
AX_X = mybir.AxisListType.X
ds = bass.ds

P = 128
D = 1024
KT = D // P
TOK = 2
S = TOK * P
HEADS = 16
DH = 64
PAIRS = HEADS // 2
FF = 2816
FFC = 256
MLPC = 512
N_FF = FF // FFC
N_MLP = 4 * D // MLPC
GROUPS = 4
GD = D // GROUPS
CHUNK = 64
EPS = 1e-6
NEG = -1e30
FAR = 1e33
RING = 8
RAW = 4
WIDE = 1024
AHEAD = 4
PV = RING // RAW

PROJ_SEMS = lambda chunks: {"pj_done": 2 * chunks}
TR = lambda sets: {"tr_ready": 4, "tr_hi": 8 * sets, "tr_lo": 8 * sets}
STAT = {"ms_done": 2, "rms_done": 2, "rstd_done": 2}
NORM = {**STAT, "xn_done": 2}


def ffn_sems(n):
    return {"act_done": 2 * n, "h_done": 2 * n, "ht_ready": 2 * n, "ht_hi": 2 * n,
            "ht_lo": 2 * n, "x_done": 4, "units": RING * n}


def att_sems(extra):
    return {"qt_done": PAIRS, "kt_done": PAIRS,
            "v_done": PAIRS, "z_ready": HEADS, "r_ready": HEADS, "w_done": HEADS, "y_ready": PAIRS,
            "y_hi": PAIRS, "y_lo": PAIRS, "units": 4 * PAIRS, **extra}


STICK = {"abs_done": HEADS, "exp_done": HEADS, "ln_done": HEADS, "sp_done": HEADS, "spm_done": HEADS,
         "wm_done": HEADS}
SOFT = {"sm_done": HEADS, "max_done": HEADS, "p_done": HEADS, "rs_done": HEADS, "pn_done": HEADS}

PHASES = [
    ("norm_ff1", {**NORM, **TR(1)}), ("ff1", ffn_sems(N_FF)),
    ("norm_mix", {**NORM, **TR(1)}), ("stick", att_sems(STICK)),
    ("a_in", {**PROJ_SEMS(4), "units": 16}), ("gates", {**PROJ_SEMS(4), "units": 16}),
    ("smix", {}),
    ("branch_b", {**PROJ_SEMS(2), "units": 8}), ("tr_a", TR(1)), ("branch_a", {**PROJ_SEMS(2), "units": 8}),
    ("tr_m", TR(1)), ("w_out", {**PROJ_SEMS(2), "units": 8, "x_done": 4}),
    ("norm_ff2", {**NORM, **TR(1)}), ("ff2", ffn_sems(N_FF)),
    ("final1", {**STAT, "x_done": 2}),
    ("norm_moba", {**NORM, **TR(1)}), ("moba", att_sems(SOFT)),
    ("w_o0", {**PROJ_SEMS(2), "units": 8, "x_done": 4}),
    ("norm_mlp0", {**NORM, **TR(1)}), ("mlp0", ffn_sems(N_MLP)),
    ("norm_fox", {**NORM, **TR(2)}), ("fox", att_sems(SOFT)),
    ("w_o1", {**PROJ_SEMS(2), "units": 8, "x_done": 4}),
    ("norm_mlp1", {**NORM, **TR(1)}), ("mlp1", ffn_sems(N_MLP)),
    ("final2", {**STAT, "x_done": 2}),
]


TURN_BANK = {name: 0 if name in ("norm_ff1", "norm_ff2", "norm_mlp0", "norm_mlp1") else 4 for name, _ in PHASES}


def begins():
    now, at = {}, {}
    for name, adds in PHASES:
        at[name] = dict(now)
        for key, n in adds.items():
            now[key] = now.get(key, 0) + n
    at["end"] = now
    return at


AT = begins()
UNITS = AT["end"]["units"]


def at(phase, key):
    return AT[phase].get(key, 0)


def unit_shapes():
    shapes = []
    for name, adds in PHASES:
        n = adds.get("units", 0)
        if name in ("ff1", "ff2"):
            shapes += [(1024, 2)] * 4
            for c in range(N_FF):
                shapes += ([(1024, 2)] * 4 if c < N_FF - 1 else []) + [(512, 1)] * 4
        elif name in ("stick", "moba", "fox"):
            shapes += [(1024, 1), (1024, 1), (512, 1), (512, 1)] * PAIRS
        else:
            shapes += [(1024, 1)] * n
    assert len(shapes) == UNITS
    return shapes


UNIT = unit_shapes()


def landed_value(c, i):
    def upto(u):
        return sum(16 * UNIT[v][1] for v in range(u % RAW, u + 1, RAW))
    if isinstance(i, int) and i == 0:
        return upto(c)
    return upto(c) + (upto(c + RING) - upto(c)) * i


def two_blocks(nc, x_in, ff1_norm, ff1_w_gate, ff1_w_up, ff1_w_down, mix_norm, w_in, b_gate, gmlp_ln_g,
               gmlp_ln_b, gmlp_w_s, gmlp_b_s, w_branch_a, w_branch_b, w_out, ff2_norm, ff2_w_gate, ff2_w_up,
               ff2_w_down, final_norm, attn_norm_2, moba_w_qkv_2, fox_w_q_2, w_o_2, kv_norm_2, w_kv_2, w_f_2,
               b_f_2, mlp_norm_2, w_up_2, w_down_2, final_norm_2, out):
    ctx = ExitStack()
    with ctx:
        def sb(name, shape, dt=F32, scope=ctx):
            return scope.enter_context(nc.sbuf_tensor(name, shape, dt))

        def sem(name):
            return ctx.enter_context(nc.semaphore(name))

        raw = sb("raw", [P, RAW, WIDE])
        w_hi = sb("w_hi", [P, RING, WIDE], F32R)
        w_lo = sb("w_lo", [P, RING, WIDE], F32R)
        x = sb("x", [P, TOK, D])
        xn = sb("xn", [P, TOK, D])
        xt_hi = sb("xt_hi", [P, KT, S], F32R)
        xt_lo = sb("xt_lo", [P, KT, S], F32R)
        yt_hi = sb("yt_hi", [P, KT, S], F32R)
        yt_lo = sb("yt_lo", [P, KT, S], F32R)
        ht_hi = sb("ht_hi", [P, 4, S], F32R)
        ht_lo = sb("ht_lo", [P, 4, S], F32R)
        work = [sb(f"work{n}", [P, 2, 512]) for n in range(3)]
        qt = sb("qt", [P, 2, S])
        kt = sb("kt", [P, 2, S])
        vn = sb("vn", [P, 2, TOK, P])
        row_gain = sb("row_gain", [P, D])
        ident = sb("ident", [P, P])
        tri = sb("tri", [P, P])
        ntri = sb("ntri", [P, P])
        ones = sb("ones", [P, P])
        nones = sb("nones", [P, P])
        zeros = sb("zeros", [P, 512], BF16)
        gain_rows = sb("gain_rows", [P, P])
        gain = sb("gain", [P, 72])
        ms = sb("ms", [P, 2])
        rms = sb("rms", [P, 2])
        eps = sb("eps", [P, 1])
        sqrt_warm = sb("sqrt_warm", [P, 1])
        rstd = sb("rstd", [P, 2])
        mx = sb("mx", [P, 2, 2])
        rsum = sb("rsum", [P, 2, 2])
        rinv = sb("rinv", [P, 2, 2])
        one = ExitStack()
        a_uv = sb("a_uv", [P, TOK, 2 * D], scope=one)
        gates = sb("gates", [P, TOK, 2 * D], scope=one)
        ln_rows = sb("ln_rows", [P, 2, D], scope=one)
        ws = sb("ws", [P, GROUPS, P], scope=one)
        wst = sb("wst", [P, GROUPS, P], scope=one)
        bn6 = sb("bn6", [P, TOK * GROUPS, 6], scope=one)
        bn2 = sb("bn2", [P, TOK * GROUPS, 2], scope=one)
        ln_rstd = sb("ln_rstd", [P, TOK * GROUPS], scope=one)
        one.close()
        two = ctx.enter_context(ExitStack())
        xq_hi = sb("xq_hi", [P, KT, S], F32R, scope=two)
        xq_lo = sb("xq_lo", [P, KT, S], F32R, scope=two)
        dist = sb("dist", [P, 3 * P], scope=two)
        dist_i = sb("dist_i", [P, 3 * P], I32, scope=two)
        mask = sb("mask", [P, 3 * P], scope=two)
        nslope = sb("nslope", [P, HEADS], scope=two)
        wf = sb("wf", [P, KT, HEADS], scope=two)
        wf_hi = sb("wf_hi", [P, KT, HEADS], F32R, scope=two)
        wf_lo = sb("wf_lo", [P, KT, HEADS], F32R, scope=two)
        bf = sb("bf", [P, HEADS], scope=two)
        fz = sb("fz", [P, TOK, HEADS], scope=two)
        fe = sb("fe", [P, TOK, HEADS], scope=two)
        logf = sb("logf", [P, TOK, HEADS], scope=two)
        cn = sb("cn", [P, TOK, HEADS], scope=two)
        ct = sb("ct", [HEADS, S], scope=two)
        c_row = sb("c_row", [1, HEADS * S], scope=two)

        bank = [ctx.enter_context(nc.psum_tensor(f"bank{n}", [P, 512], F32)) for n in range(8)]
        gu_bank, t_bank = bank[4:6], bank[6:8]
        q_bank, k_bank, v_bank, y_bank = bank[0:4]
        z_bank = bank[4:6]

        landed = [sem(f"landed{n}") for n in range(RAW)]
        s = {name: sem(name) for name in (
            "hi_ready", "lo_ready", "used",
            "x_in", "rows_in", "gain_in", "gain_ready", "gain_cols", "blk1_in", "ws_ready", "wst_done", "ws_in",
            "pool_turns", "sp_turns", "const_done", "const2_done", "gate_in", "wf_in", "row2_in", "zero_done",
            "ms_done", "rms_done", "rstd_done", "xn_done", "tr_ready", "tr_hi", "tr_lo",
            "act_done", "h_done", "ht_ready", "ht_hi", "ht_lo", "x_done",
            "qt_done", "kt_done", "v_done", "z_ready", "r_ready",
            "abs_done", "exp_done", "ln_done", "sp_done", "spm_done", "w_done", "wm_done",
            "y_ready", "y_hi", "y_lo", "sm_done", "max_done", "p_done", "rs_done", "pn_done",
            "pj_done", "gelu_done", "gate_done", "bn_done", "bna_done", "lns_done", "lnr_done", "ln_done2",
            "lng_done", "v_ln", "smix_ready", "ya_done", "prod_done", "m_done",
            "wf_hi_done", "wf_lo_done", "f_ready", "fz_done", "fabs_done", "fexp_done", "fln_done", "logf_done",
            "c_ready", "ct_done", "cn_done", "c_row_in", "stored")}

        def tiles(w):
            return w.rearrange("(k p) n -> p k n", p=P)

        win, wba, wbb, wout = (tiles(w[0]) for w in (w_in, w_branch_a, w_branch_b, w_out))
        qkv_moba = [tiles(moba_w_qkv_2[0])[:, :, n * D:(n + 1) * D] for n in range(3)]
        kv = tiles(w_kv_2)
        qkv_fox = [tiles(fox_w_q_2[0]), kv[:, :, 0:D], kv[:, :, D:2 * D]]
        qkv_stick = [win[:, :, (2 + n) * D:(3 + n) * D] for n in range(3)]
        wo = [tiles(w_o_2[n]) for n in range(2)]

        def ht_of(buf, t, t_cols):
            if t_cols == S:
                return buf[:, t, :]
            return buf[:, 2 * t:2 * t + 2, :].rearrange("p a b -> p (a b)")

        def consumed(eng, c, i=0):
            eng.wait_ge(s["used"], RING + c + 1 + RING * i)

        block = ctx.enter_context(nc.Block())

        @block.sync
        def _(sp):
            def room(c, i):
                sp.wait_ge(s["lo_ready"], RING + c - RAW + 1 + RING * i)

            def send(c, i, dst, src):
                sp.dma_start(dst, src).then_inc(landed[c % RAW], 16)

            def slot(c, k, w):
                return raw[:, c % RAW, 0:w].rearrange("p (k n) -> p k n", k=k)

            def ff_units(phase, w_gate, w_up, w_down):
                b = at(phase, "units")
                wg, wu, wd = tiles(w_gate[0]), tiles(w_up[0]), tiles(w_down[0])

                def gate_up(c, i, chunk):
                    for j in range(4):
                        room(c + j, i)
                        for half, w in enumerate((wg, wu)):
                            send(c + j, i, slot(c + j, 2, 1024)[:, :, half * FFC:(half + 1) * FFC],
                                 w[:, 2 * j:2 * j + 2, ds(chunk * FFC, FFC)])

                def down(c, i, chunk):
                    for j in range(4):
                        room(c + j, i)
                        send(c + j, i, slot(c + j, 1, 512),
                             wd[:, ds(2 * chunk + j // 2, 1), (j % 2) * 512:(j % 2) * 512 + 512])

                gate_up(b, 0, 0)
                with sp.Fori(0, N_FF - 1) as i:
                    gate_up(b + 4, i, i + 1)
                    down(b + 8, i, i)
                down(b + RING * N_FF - 4, 0, N_FF - 1)

            def mlp_units(phase, w_up, w_down):
                b = at(phase, "units")
                wu, wd = tiles(w_up), tiles(w_down)

                def up(c, i, chunk):
                    for j in range(4):
                        room(c + j, i)
                        send(c + j, i, slot(c + j, 2, 1024), wu[:, 2 * j:2 * j + 2, ds(chunk * MLPC, MLPC)])

                def down(c, i, chunk):
                    for j in range(4):
                        room(c + j, i)
                        send(c + j, i, slot(c + j, 1, 1024), wd[:, ds(4 * chunk + j, 1), :])

                up(b, 0, 0)
                with sp.Fori(0, N_MLP - 1) as i:
                    up(b + 4, i, i + 1)
                    down(b + 8, i, i)
                down(b + RING * N_MLP - 4, 0, N_MLP - 1)

            def pair_units(phase, qkv):
                b = at(phase, "units")

                def pair(c, i, pr):
                    cols = ds(pr * P, P)
                    for j in range(2):
                        room(c + j, i)
                        send(c + j, i, slot(c + j, KT, 1024), qkv[j][:, :, cols])
                    for j in range(2):
                        room(c + 2 + j, i)
                        send(c + 2 + j, i, slot(c + 2 + j, 4, 512), qkv[2][:, 4 * j:4 * j + 4, cols])

                with sp.Fori(0, PAIRS // 2) as i:
                    pair(b, i, 2 * i)
                    pair(b + 4, i, 2 * i + 1)

            def proj_units(phase, w, col):
                b, n = at(phase, "units"), dict(PHASES)[phase]["units"] // RING

                def body(i, first):
                    for e in range(2):
                        for j in range(4):
                            c = b + 4 * e + j
                            room(c, i)
                            if n > 1 and e == 0 and j == 0:
                                sp.sem_inc(s["sp_turns"], 1)
                            send(c, i, slot(c, 2, 1024), w[:, 2 * j:2 * j + 2, ds(first + 512 * e, 512)])
                if n == 1:
                    body(0, 0)
                else:
                    with sp.Fori(0, n) as i:
                        body(i, sp.snap(col(i)))

            ff_units("ff1", ff1_w_gate, ff1_w_up, ff1_w_down)
            pair_units("stick", qkv_stick)
            proj_units("a_in", win, lambda i: D - D * i)
            proj_units("gates", win, lambda i: 5 * D + D * i)
            proj_units("branch_b", wbb, lambda i: 0)
            proj_units("branch_a", wba, lambda i: 0)
            proj_units("w_out", wout, lambda i: 0)
            ff_units("ff2", ff2_w_gate, ff2_w_up, ff2_w_down)
            pair_units("moba", qkv_moba)
            proj_units("w_o0", wo[0], lambda i: 0)
            mlp_units("mlp0", w_up_2[0], w_down_2[0])
            pair_units("fox", qkv_fox)
            proj_units("w_o1", wo[1], lambda i: 0)
            mlp_units("mlp1", w_up_2[1], w_down_2[1])
            for tok in range(TOK):
                sp.wait_ge(s["x_done"], at("final2", "x_done") + tok + 1)
                sp.dma_start(out[0, tok * P:(tok + 1) * P, :], x[:, tok, :]).then_inc(s["stored"], 16)
            sp.wait_ge(s["stored"], 16 * TOK)

        @block.gpsimd
        def _(pool):
            count = {"n": 0}

            def const(ins, name="const_done"):
                ins.then_inc(s[name], 1)
                count["n"] += 1
                pool.wait_ge(s[name], count["n"])

            pool.memset(zeros[:], 0.0).then_inc(s["zero_done"], 1)
            pool.memset(eps[:], EPS).then_inc(s["zero_done"], 1)
            const(pool.memset(ident[:], 0.0))
            const(pool.affine_select(out=ident[:], in_=ident[:], compare_op=ALU.not_equal, fill=1.0, base=0,
                                     pattern=[[-1, P]], channel_multiplier=1))
            const(pool.memset(ones[:], 1.0))
            const(pool.memset(nones[:], -1.0))
            const(pool.affine_select(out=tri[:], in_=ones[:], compare_op=ALU.is_ge, fill=0.0, base=0,
                                     pattern=[[1, P]], channel_multiplier=-1))
            const(pool.affine_select(out=ntri[:], in_=nones[:], compare_op=ALU.is_ge, fill=0.0, base=0,
                                     pattern=[[-1, P]], channel_multiplier=1))
            consumed(pool, 3)
            pool.dma_start(ln_rows[:, 0, :], gmlp_ln_g.rearrange("a g c -> a (g c)").broadcast_to([P, D]))\
                .then_inc(s["blk1_in"], 16)
            pool.dma_start(ln_rows[:, 1, :], gmlp_ln_b.rearrange("a g c -> a (g c)").broadcast_to([P, D]))\
                .then_inc(s["blk1_in"], 16)
            for tok in range(TOK):
                pool.dma_start(gates[:, tok, :], b_gate.broadcast_to([P, 2 * D])).then_inc(s["gate_in"], 16)
            pool.dma_start(row_gain[:], final_norm.rearrange("(a n) -> a n", a=1).broadcast_to([P, D]))\
                .then_inc(s["rows_in"], 16)

            def causal(buf, h):
                v = buf[:, h, 0:512].rearrange("p (b t) -> p b t", b=2)[:, :, 0:P]
                return pool.affine_select(out=v, in_=v, compare_op=ALU.is_gt, fill=0.0, base=0,
                                          pattern=[[0, 2], [1, P]], channel_multiplier=-1)

            with pool.Fori(0, PAIRS) as pr:
                for h in range(2):
                    pool.wait_ge(s["sp_done"], 2 * pr + h + 1)
                    pool.sem_inc(s["pool_turns"], 1)
                    causal(work[1], h).then_inc(s["spm_done"], 1)
                for h in range(2):
                    pool.wait_ge(s["w_done"], 2 * pr + h + 1)
                    pool.sem_inc(s["pool_turns"], 1)
                    causal(work[2], h).then_inc(s["wm_done"], 1)

            pool.wait_ge(s["blk1_in"], 32)
            for tok in range(TOK):
                v = a_uv[:, tok, 0:D]
                pool.wait_ge(s["ln_done2"], GROUPS * (tok + 1))
                pool.tensor_tensor(v, v, ln_rows[:, 0, :], ALU.mult).then_inc(s["lng_done"], 1)
                pool.wait_ge(s["lng_done"], tok + 1)
                pool.tensor_tensor(v, v, ln_rows[:, 1, :], ALU.add).then_inc(s["v_ln"], 1)

            pool.wait_ge(s["x_done"], at("norm_ff2", "x_done"))
            count["n"] = 0
            for t, base in ((0, 0), (P, P)):
                const(pool.iota(dist_i[:, t:t + P + base], pattern=[[-1, P + base]], base=base,
                                channel_multiplier=1), "const2_done")
            const(pool.tensor_copy(dist[:], dist_i[:]), "const2_done")
            const(pool.memset(mask[:], 0.0), "const2_done")
            for t, base in ((0, 0), (P, P)):
                for buf, fill in ((dist, FAR), (mask, NEG)):
                    v = buf[:, t:t + P + base]
                    const(pool.affine_select(out=v, in_=v, compare_op=ALU.is_ge, fill=fill, base=base,
                                             pattern=[[-1, P + base]], channel_multiplier=1), "const2_done")
            for h in range(HEADS):
                const(pool.memset(nslope[:, h:h + 1], -float(np.float32(2.0 ** (-8.0 * (h + 1) / HEADS)))),
                      "const2_done")
            pool.dma_start(wf[:], tiles(w_f_2)).then_inc(s["wf_in"], 16)
            pool.dma_start(bf[:], b_f_2.rearrange("(a n) -> a n", a=1).broadcast_to([P, HEADS]))\
                .then_inc(s["wf_in"], 16)
            pool.wait_ge(s["x_done"], at("norm_moba", "x_done"))
            pool.dma_start(row_gain[:], final_norm_2.rearrange("(a n) -> a n", a=1).broadcast_to([P, D]))\
                .then_inc(s["row2_in"], 16)
            pool.wait_ge(s["ct_done"], 1)
            pool.dma_start(c_row[:].rearrange("a (h t) -> a h t", h=HEADS), ct[:]).then_inc(s["c_row_in"], 16)

        @block.scalar
        def _(act):
            for tok in range(TOK):
                act.dma_start(x[:, tok, :], x_in[0, tok * P:(tok + 1) * P, :]).then_inc(s["x_in"], 16)
            rows = [ff1_norm[0:1], mix_norm[0:1], ff2_norm[0:1], attn_norm_2[0:1], attn_norm_2[1:2],
                    mlp_norm_2[0:1], mlp_norm_2[1:2], kv_norm_2.rearrange("(a n) -> a n", a=1)]
            for n, g in enumerate(rows):
                act.dma_start(gain_rows[8 * n:8 * n + 8, :], g.rearrange("a (k p) -> (a k) p", p=P))\
                    .then_inc(s["gain_in"], 16)
            act.dma_start(gain_rows[64:64 + GROUPS, :], gmlp_b_s[0]).then_inc(s["gain_in"], 16)
            act.dma_start(ws[:], gmlp_w_s[0].rearrange("g t s -> t g s")).then_inc(s["ws_in"], 16)

            def hi(c, i=0):
                if c >= UNITS:
                    return
                w = UNIT[c][0]
                act.wait_ge(landed[c % RAW], landed_value(c, i))
                act.wait_ge(s["used"], c + 1 + RING * i)
                act.activation(w_hi[:, c % RING, 0:w], raw[:, c % RAW, 0:w], ACT.Copy).then_inc(s["hi_ready"], 1)

            def stat(phase, x_value):
                act.activation(sqrt_warm[:], eps[:], ACT.Sqrt)
                for tok in range(TOK):
                    if x_value is None:
                        act.wait_ge(s["x_in"], 32)
                    else:
                        act.wait_ge(s["x_done"], x_value(tok))
                    act.activation(xn[:, tok, :], x[:, tok, :], ACT.Square, scale=1.0 / 32.0,
                                   accum_out=ms[:, tok:tok + 1]).then_inc(s["ms_done"], 1)
                    act.wait_ge(s["ms_done"], at(phase, "ms_done") + tok + 1)
                    act.activation(rms[:, tok:tok + 1], ms[:, tok:tok + 1], ACT.Sqrt, bias=eps[:])\
                        .then_inc(s["rms_done"], 1)

            def transposed(phase, sets):
                for b in range(4):
                    act.wait_ge(s["tr_ready"], at(phase, "tr_ready") + b + 1)
                    for k in (2 * b, 2 * b + 1):
                        for dst, g in sets:
                            src = bank[TURN_BANK[phase] + b][:, (k % 2) * S:(k % 2 + 1) * S]
                            if g is None:
                                act.activation(dst[:, k, :], src, ACT.Copy).then_inc(s["tr_hi"], 1)
                            else:
                                act.activation(dst[:, k, :], src, ACT.Copy,
                                               scale=gain[:, 8 * g + k:8 * g + k + 1]).then_inc(s["tr_hi"], 1)

            def ffn(phase, n, func, width, t_cols):
                b = at(phase, "units")

                def chunk(c, i, m, last_up):
                    hi(c + 4, i)
                    hi(c + 5, i)
                    for tok in range(TOK):
                        consumed(act, last_up, i)
                        act.activation(work[0][:, tok, 0:width], gu_bank[tok][:, 0:width], func)\
                            .then_inc(s["act_done"], 1)
                    for u in range(6, 10):
                        hi(c + u, i)
                    for t in range(2):
                        act.wait_ge(s["ht_ready"], at(phase, "ht_ready") + 2 * m + t + 1)
                        act.activation(ht_of(ht_hi, t, t_cols), t_bank[t][:, 0:t_cols], ACT.Copy)\
                            .then_inc(s["ht_hi"], 1)
                    hi(c + 10, i)
                    hi(c + 11, i)

                chunk(b, 0, 0, b + 3)
                with act.Fori(1, n - 1) as i:
                    chunk(b, i, i, b - 1)
                chunk(b + RING * (n - 1), 0, n - 1, b + RING * (n - 1) - 1)

            def v_evac(c, i, e):
                consumed(act, c + 3, i)
                act.activation(vn[:, e, :, :], v_bank[:, 0:S].rearrange("p (t n) -> p t n", t=TOK), ACT.Copy)\
                    .then_inc(s["v_done"], 1)

            def q_evac(c, i, e):
                consumed(act, c, i)
                act.activation(qt[:, e, :], q_bank[:, 0:S], ACT.Copy, scale=0.125).then_inc(s["qt_done"], 1)

            def attention(phase, soft):
                b = at(phase, "units")
                hp = at(phase, "z_ready")
                own = at(phase, "sm_done" if soft else "abs_done")

                def first_part(pr):
                    for h in range(2):
                        if soft:
                            for t in range(TOK):
                                if t == 0:
                                    act.wait_ge(s["max_done"], own + 2 * pr + h + 1)
                                cols = slice(0, P) if t == 0 else slice(P, 3 * P)
                                ins = act.activation(work[1][:, h, cols], work[0][:, h, cols], ACT.Exp,
                                                     bias=mx[:, h, t:t + 1], accum_out=rsum[:, h, t:t + 1])
                            ins.then_inc(s["p_done"], 1)
                        else:
                            act.wait_ge(s["z_ready"], hp + 2 * pr + h + 1)
                            act.activation(work[0][:, h, 0:3 * P], z_bank[h][:, 0:3 * P], ACT.Abs)\
                                .then_inc(s["abs_done"], 1)
                            act.wait_ge(s["abs_done"], own + 2 * pr + h + 1)
                            act.activation(work[0][:, h, 0:3 * P], work[0][:, h, 0:3 * P], ACT.Exp, scale=-1.0)\
                                .then_inc(s["exp_done"], 1)
                    if not soft:
                        for h in range(2):
                            act.wait_ge(s["exp_done"], own + 2 * pr + h + 1)
                            act.activation(work[0][:, h, 0:3 * P], work[0][:, h, 0:3 * P], ACT.Ln, bias=1.0)\
                                .then_inc(s["ln_done"], 1)

                def second_part(pr):
                    for h in range(2):
                        act.wait_ge(s["r_ready"], hp + 2 * pr + h + 1)
                        src = t_bank[h] if soft else z_bank[h]
                        act.activation(work[2][:, h, 0:3 * P], src[:, 0:3 * P], ACT.Copy if soft else ACT.Exp)\
                            .then_inc(s["w_done"], 1)

                def y_part(pr):
                    act.wait_ge(s["y_ready"], at(phase, "y_ready") + pr + 1)
                    act.activation(yt_hi[:, ds(pr, 1), :], y_bank[:, 0:S], ACT.Copy).then_inc(s["y_hi"], 1)

                def period(c, i, pr, e):
                    first_part(pr)
                    hi(c + 8, i)
                    q_evac(c + 4, i, 1 - e)
                    hi(c + 9, i)
                    hi(c + 10, i)
                    second_part(pr)
                    hi(c + 11, i)
                    v_evac(c + 4, i, 1 - e)
                    y_part(pr)

                hi(b + 4)
                q_evac(b, 0, 0)
                for u in (5, 6, 7):
                    hi(b + u)
                v_evac(b, 0, 0)
                with act.Fori(0, PAIRS // 2 - 1) as i:
                    period(b, i, 2 * i, 0)
                    period(b + 4, i, 2 * i + 1, 1)
                period(b + 4 * (PAIRS - 2), 0, PAIRS - 2, 0)
                first_part(PAIRS - 1)
                second_part(PAIRS - 1)
                y_part(PAIRS - 1)

            def chunks(phase, evac=None):
                b, n = at(phase, "units"), dict(PHASES)[phase]["units"] // RING

                def body(i):
                    for e in range(2):
                        for j in range(4):
                            hi(b + 4 * e + AHEAD + j, i)
                        if evac:
                            evac(2 * i + e, e, b + 4 * e + 3, i)
                if n == 1:
                    body(0)
                else:
                    with act.Fori(0, n - 1) as i:
                        body(i)
                    b += RING * (n - 1)
                    for e in range(2):
                        for j in range(4):
                            hi(b + 4 * e + AHEAD + j)
                        if evac:
                            evac(2 * (n - 1) + e, e, b + 4 * e + 3, 0)

            def gelu(m, e, c, i):
                for tok in range(TOK):
                    consumed(act, c, i)
                    act.activation(a_uv[:, tok, ds(m * 512, 512)], bank[2 * e + tok][:], ACT.Gelu)\
                        .then_inc(s["pj_done"], 1)

            def sigmoid(m, e, c, i):
                for tok in range(TOK):
                    act.wait_ge(s["pj_done"], at("gates", "pj_done") + 2 * m + tok + 1)
                    g = gates[:, tok, ds(m * 512, 512)]
                    act.activation(g, g, ACT.Sigmoid).then_inc(s["gate_done"], 1)

            def after_x(phase, tok_first):
                total = at(phase, "x_done")
                return lambda tok: total - (2 if tok_first and tok == 0 else 0)

            for u in range(AHEAD):
                hi(u)
            act.wait_ge(s["zero_done"], 2)
            stat("norm_ff1", None)
            act.wait_ge(s["gain_cols"], 1)
            transposed("norm_ff1", [(xt_hi, 0)])
            ffn("ff1", N_FF, ACT.Silu, FFC, S)
            stat("norm_mix", after_x("norm_mix", True))
            transposed("norm_mix", [(xt_hi, 1)])
            attention("stick", False)
            chunks("a_in", gelu)
            act.wait_ge(s["bna_done"], TOK * GROUPS)
            act.activation(ln_rstd[:], bn2[:, :, 1], ACT.Sqrt, bias=eps[:]).then_inc(s["lns_done"], 1)
            chunks("gates", sigmoid)
            for e in range(2):
                for j in range(4):
                    hi(at("branch_b", "units") + 4 * e + AHEAD + j)
                if e == 0:
                    transposed("tr_a", [(xt_hi, None)])
            chunks("branch_a")
            transposed("tr_m", [(yt_hi, None)])
            chunks("w_out")
            stat("norm_ff2", after_x("norm_ff2", False))
            transposed("norm_ff2", [(xt_hi, 2)])
            ffn("ff2", N_FF, ACT.Silu, FFC, S)
            stat("final1", after_x("final1", True))
            stat("norm_moba", lambda tok: at("norm_moba", "x_done") - 1 + tok)
            transposed("norm_moba", [(xt_hi, 3)])
            attention("moba", True)
            chunks("w_o0")
            stat("norm_mlp0", after_x("norm_mlp0", False))
            transposed("norm_mlp0", [(xt_hi, 5)])
            ffn("mlp0", N_MLP, ACT.Relu, MLPC, 2 * S)
            act.wait_ge(s["wf_in"], 32)
            act.activation(wf_hi[:], wf[:], ACT.Copy).then_inc(s["wf_hi_done"], 1)
            stat("norm_fox", after_x("norm_fox", True))
            transposed("norm_fox", [(xt_hi, 7), (xq_hi, 4)])
            act.wait_ge(s["fz_done"], 1)
            act.activation(fe[:], fz[:], ACT.Abs).then_inc(s["fabs_done"], 1)
            act.wait_ge(s["fabs_done"], 1)
            act.activation(fe[:], fe[:], ACT.Exp, scale=-1.0).then_inc(s["fexp_done"], 1)
            act.wait_ge(s["fexp_done"], 1)
            act.activation(fe[:], fe[:], ACT.Ln, bias=1.0).then_inc(s["fln_done"], 1)
            attention("fox", True)
            chunks("w_o1")
            stat("norm_mlp1", after_x("norm_mlp1", False))
            transposed("norm_mlp1", [(xt_hi, 6)])
            ffn("mlp1", N_MLP, ACT.Relu, MLPC, 2 * S)
            stat("final2", after_x("final2", True))

        @block.vector
        def _(dve):
            def lo(c, i=0):
                if c >= UNITS:
                    return
                w = UNIT[c][0]
                dve.wait_ge(s["hi_ready"], c + 1 + RING * i)
                dve.tensor_tensor(w_lo[:, c % RING, 0:w], raw[:, c % RAW, 0:w],
                                  w_hi[:, c % RING, 0:w].bitcast(F32), ALU.subtract).then_inc(s["lo_ready"], 1)

            def root(phase, tok):
                dve.wait_ge(s["rms_done"], at(phase, "rms_done") + tok + 1)
                dve.reciprocal(rstd[:, tok:tok + 1], rms[:, tok:tok + 1])\
                    .then_inc(s["rstd_done"], 1)
                dve.wait_ge(s["rstd_done"], at(phase, "rstd_done") + tok + 1)

            def norm(phase):
                for tok in range(TOK):
                    root(phase, tok)
                    dve.tensor_scalar(xn[:, tok, :], x[:, tok, :], rstd[:, tok:tok + 1], None, ALU.mult)\
                        .then_inc(s["xn_done"], 1)

            def final(phase):
                for tok in range(TOK):
                    root(phase, tok)
                    dve.scalar_tensor_tensor(x[:, tok, :], x[:, tok, :], rstd[:, tok:tok + 1], row_gain[:],
                                             ALU.mult, ALU.mult).then_inc(s["x_done"], 1)

            def transposed(phase, sets):
                for k in range(KT):
                    dve.wait_ge(s["tr_hi"], at(phase, "tr_hi") + len(sets) * (k + 2 - k % 2))
                    for low, high, g in sets:
                        src = bank[TURN_BANK[phase] + k // 2][:, (k % 2) * S:(k % 2 + 1) * S]
                        if g is None:
                            dve.tensor_tensor(low[:, k, :], src, high[:, k, :].bitcast(F32), ALU.subtract)\
                                .then_inc(s["tr_lo"], 1)
                        else:
                            dve.scalar_tensor_tensor(low[:, k, :], src, gain[:, 8 * g + k:8 * g + k + 1],
                                                     high[:, k, :].bitcast(F32), ALU.mult, ALU.subtract)\
                                .then_inc(s["tr_lo"], 1)

            def ffn(phase, n, width, off, t_cols):
                b = at(phase, "units")

                def chunk(c, i, m):
                    lo(c + 4, i)
                    lo(c + 5, i)
                    for tok in range(TOK):
                        dve.wait_ge(s["act_done"], at(phase, "act_done") + 2 * m + tok + 1)
                        dve.tensor_tensor(work[1][:, tok, 0:width], work[0][:, tok, 0:width],
                                          gu_bank[tok][:, off:off + width] if off else work[0][:, tok, 0:width],
                                          ALU.mult).then_inc(s["h_done"], 1)
                    for u in range(6, 10):
                        lo(c + u, i)
                    for t in range(2):
                        dve.wait_ge(s["ht_hi"], at(phase, "ht_hi") + 2 * m + t + 1)
                        dve.tensor_tensor(ht_of(ht_lo, t, t_cols), t_bank[t][:, 0:t_cols],
                                          ht_of(ht_hi, t, t_cols).bitcast(F32), ALU.subtract)\
                            .then_inc(s["ht_lo"], 1)
                    lo(c + 10, i)
                    lo(c + 11, i)

                with dve.Fori(0, n - 1) as i:
                    chunk(b, i, i)
                chunk(b + RING * (n - 1), 0, n - 1)

            def add_residual(phase, scale):
                for tok in range(TOK):
                    consumed(dve, at(phase, "units") + dict(PHASES)[phase]["units"] - 1)
                    for half in range(2):
                        v = x[:, tok, half * 512:(half + 1) * 512]
                        dve.scalar_tensor_tensor(v, bank[2 * tok + half][:], scale, v, ALU.mult, ALU.add)\
                            .then_inc(s["x_done"], 1)

            def k_evac(c, i, e):
                consumed(dve, c + 1, i)
                dve.tensor_copy(kt[:, e, :], k_bank[:, 0:S]).then_inc(s["kt_done"], 1)

            def attention(phase, kind):
                b = at(phase, "units")
                hp = at(phase, "z_ready")
                own = at(phase, "abs_done" if kind == "stick" else "sm_done")

                def first_part(pr):
                    for h in range(2):
                        if kind == "stick":
                            break
                        dve.wait_ge(s["z_ready"], hp + 2 * pr + h + 1)
                        a, z = work[0][:, h, 0:3 * P], z_bank[h][:, 0:3 * P]
                        if kind == "moba":
                            dve.scalar_tensor_tensor(a, dist[:], nslope[:, ds(2 * pr + h, 1)], z,
                                                     ALU.mult, ALU.add).then_inc(s["sm_done"], 1)
                        else:
                            dve.scalar_tensor_tensor(a[:, 0:P], z[:, 0:P], cn[:, 0, ds(2 * pr + h, 1)],
                                                     mask[:, 0:P], ALU.add, ALU.add)
                            dve.scalar_tensor_tensor(a[:, P:3 * P], z[:, P:3 * P], cn[:, 1, ds(2 * pr + h, 1)],
                                                     mask[:, P:3 * P], ALU.add, ALU.add)\
                                .then_inc(s["sm_done"], 1)
                    if kind != "stick":
                        for h in range(2):
                            dve.wait_ge(s["sm_done"], own + 2 * pr + h + 1)
                            dve.tensor_reduce(mx[:, h, 0:1], work[0][:, h, 0:P], AX_X, ALU.max, negate=True)
                            dve.tensor_reduce(mx[:, h, 1:2], work[0][:, h, P:3 * P], AX_X, ALU.max, negate=True)\
                                .then_inc(s["max_done"], 1)

                def second_part(pr):
                    for h in range(2):
                        if kind == "stick":
                            dve.wait_ge(s["ln_done"], own + 2 * pr + h + 1)
                            dve.scalar_tensor_tensor(work[1][:, h, 0:3 * P], z_bank[h][:, 0:3 * P], 0.0,
                                                     work[0][:, h, 0:3 * P], ALU.max, ALU.add)\
                                .then_inc(s["sp_done"], 1)
                        else:
                            dve.wait_ge(s["p_done"], own + 2 * pr + h + 1)
                            dve.reciprocal(rinv[:, h, :], rsum[:, h, :]).then_inc(s["rs_done"], 1)
                            dve.wait_ge(s["rs_done"], own + 2 * pr + h + 1)
                            for t, cols in ((0, slice(0, P)), (1, slice(P, 3 * P))):
                                v = work[1][:, h, cols]
                                ins = dve.tensor_scalar(v, v, rinv[:, h, t:t + 1], None, ALU.mult)
                            ins.then_inc(s["pn_done"], 1)

                def y_part(pr):
                    dve.wait_ge(s["y_hi"], at(phase, "y_hi") + pr + 1)
                    dve.tensor_tensor(yt_lo[:, ds(pr, 1), :], y_bank[:, 0:S],
                                      yt_hi[:, ds(pr, 1), :].bitcast(F32), ALU.subtract).then_inc(s["y_lo"], 1)

                def period(c, i, pr, e):
                    first_part(pr)
                    lo(c + 8, i)
                    second_part(pr)
                    lo(c + 9, i)
                    k_evac(c + 4, i, 1 - e)
                    lo(c + 10, i)
                    lo(c + 11, i)
                    y_part(pr)

                for u in (4, 5):
                    lo(b + u)
                k_evac(b, 0, 0)
                for u in (6, 7):
                    lo(b + u)
                with dve.Fori(0, PAIRS // 2 - 1) as i:
                    period(b, i, 2 * i, 0)
                    period(b + 4, i, 2 * i + 1, 1)
                period(b + 4 * (PAIRS - 2), 0, PAIRS - 2, 0)
                first_part(PAIRS - 1)
                second_part(PAIRS - 1)
                y_part(PAIRS - 1)

            def chunks(phase, evac=None):
                b, n = at(phase, "units"), dict(PHASES)[phase]["units"] // RING

                def body(b, i, m0):
                    for e in range(2):
                        for j in range(4):
                            lo(b + 4 * e + AHEAD + j, i)
                        if evac:
                            evac(m0 + e, e, b + 4 * e + 3, i)
                if n > 1:
                    with dve.Fori(0, n - 1) as i:
                        body(b, i, 2 * i)
                body(b + RING * (n - 1), 0, 2 * (n - 1))

            def gate_bias(m, e, c, i):
                for tok in range(TOK):
                    consumed(dve, c, i)
                    g = gates[:, tok, ds(m * 512, 512)]
                    dve.tensor_tensor(g, bank[2 * e + tok][:], g, ALU.add).then_inc(s["pj_done"], 1)

            def gated(phase, half):
                def evac(m, e, c, i):
                    for tok in range(TOK):
                        consumed(dve, c, i)
                        g = gates[:, tok, half * D + m * 512:half * D + (m + 1) * 512]
                        v = xn[:, tok, m * 512:(m + 1) * 512]
                        if half:
                            dve.tensor_tensor(v, bank[2 * e + tok][:], g, ALU.mult).then_inc(s["pj_done"], 1)
                        else:
                            t = work[1][:, tok, :]
                            dve.tensor_tensor(t, bank[2 * e + tok][:], g, ALU.mult).then_inc(s["pj_done"], 1)
                            dve.wait_ge(s["pj_done"], at(phase, "pj_done") + 2 * m + tok + 1)
                            dve.tensor_tensor(v, v, t, ALU.add).then_inc(s["m_done"], 1)
                return evac

            def residual(phase):
                def evac(m, e, c, i):
                    for tok in range(TOK):
                        consumed(dve, c, i)
                        v = x[:, tok, m * 512:(m + 1) * 512]
                        dve.tensor_tensor(v, bank[2 * e + tok][:], v, ALU.add).then_inc(s["x_done"], 1)
                return evac

            dve.sem_inc(s["lo_ready"], RING)
            for u in range(AHEAD):
                lo(u)
            dve.wait_ge(s["gain_ready"], 1)
            dve.tensor_copy(gain[:, 0:68], bank[0][:, 0:68]).then_inc(s["gain_cols"], 1)
            dve.wait_ge(s["ws_ready"], 1)
            w3 = bank[1][:].rearrange("p (g t) -> p g t", g=GROUPS)
            dve.memset(wst[CHUNK:P, :, 0:CHUNK], 0.0)
            dve.tensor_copy(wst[0:CHUNK, :, :], w3[0:CHUNK, :, :])
            dve.tensor_copy(wst[CHUNK:P, :, CHUNK:P], w3[CHUNK:P, :, CHUNK:P]).then_inc(s["wst_done"], 1)
            norm("norm_ff1")
            dve.wait_ge(s["gain_cols"], 1)
            transposed("norm_ff1", [(xt_lo, xt_hi, 0)])
            ffn("ff1", N_FF, FFC, FFC, S)
            add_residual("ff1", 0.5)
            norm("norm_mix")
            transposed("norm_mix", [(xt_lo, xt_hi, 1)])
            attention("stick", "stick")
            chunks("a_in")
            for n in range(TOK * GROUPS):
                tok, g = divmod(n, GROUPS)
                dve.wait_ge(s["pj_done"], at("a_in", "pj_done") + 4)
                dve.bn_stats(bn6[:, n, :], a_uv[:, tok, g * GD:(g + 1) * GD]).then_inc(s["bn_done"], 1)
            for n in range(TOK * GROUPS):
                dve.wait_ge(s["bn_done"], n + 1)
                dve.bn_aggr(bn2[:, n, :], bn6[:, n, :]).then_inc(s["bna_done"], 1)
            dve.wait_ge(s["lns_done"], 1)
            dve.reciprocal(ln_rstd[:], ln_rstd[:]).then_inc(s["lnr_done"], 1)
            dve.wait_ge(s["lnr_done"], 1)
            for n in range(TOK * GROUPS):
                tok, g = divmod(n, GROUPS)
                v = a_uv[:, tok, g * GD:(g + 1) * GD]
                dve.tensor_scalar(v, v, bn2[:, n, 0:1], ln_rstd[:, n:n + 1], ALU.subtract, ALU.mult)\
                    .then_inc(s["ln_done2"], 1)
            dve.wait_ge(s["gate_in"], 32)
            chunks("gates", gate_bias)
            for n in range(TOK * GROUPS):
                tok, g = divmod(n, GROUPS)
                if g % 2 == 0:
                    dve.wait_ge(s["smix_ready"], n // 2 + 1)
                u = a_uv[:, tok, D + g * GD:D + (g + 1) * GD]
                dve.scalar_tensor_tensor(u, bank[4 + 2 * tok + g // 2][:, (g % 2) * GD:(g % 2 + 1) * GD],
                                         gain[:, 64 + g:65 + g], u, ALU.add, ALU.mult).then_inc(s["ya_done"], 1)
            dve.wait_ge(s["gate_done"], 8)
            evac_b = gated("branch_b", 1)
            for e in range(2):
                for j in range(4):
                    lo(at("branch_b", "units") + 4 * e + AHEAD + j)
                evac_b(e, e, at("branch_b", "units") + 4 * e + 3, 0)
                if e == 0:
                    transposed("tr_a", [(xt_lo, xt_hi, None)])
            dve.wait_ge(s["pj_done"], at("branch_a", "pj_done"))
            chunks("branch_a", gated("branch_a", 0))
            transposed("tr_m", [(yt_lo, yt_hi, None)])
            chunks("w_out", residual("w_out"))
            norm("norm_ff2")
            transposed("norm_ff2", [(xt_lo, xt_hi, 2)])
            ffn("ff2", N_FF, FFC, FFC, S)
            add_residual("ff2", 0.5)
            dve.wait_ge(s["rows_in"], 16)
            final("final1")
            norm("norm_moba")
            transposed("norm_moba", [(xt_lo, xt_hi, 3)])
            dve.wait_ge(s["const2_done"], 8 + HEADS)
            attention("moba", "moba")
            chunks("w_o0", residual("w_o0"))
            norm("norm_mlp0")
            transposed("norm_mlp0", [(xt_lo, xt_hi, 5)])
            ffn("mlp0", N_MLP, MLPC, 0, 2 * S)
            add_residual("mlp0", 1.0)
            dve.wait_ge(s["wf_hi_done"], 1)
            dve.tensor_tensor(wf_lo[:], wf[:], wf_hi[:].bitcast(F32), ALU.subtract).then_inc(s["wf_lo_done"], 1)
            norm("norm_fox")
            transposed("norm_fox", [(xt_lo, xt_hi, 7), (xq_lo, xq_hi, 4)])
            dve.wait_ge(s["f_ready"], 1)
            for tok in range(TOK):
                ins = dve.tensor_tensor(fz[:, tok, :], t_bank[0][:, tok * HEADS:(tok + 1) * HEADS], bf[:], ALU.add)
            ins.then_inc(s["fz_done"], 1)
            dve.wait_ge(s["fln_done"], 1)
            dve.scalar_tensor_tensor(logf[:], fz[:], 0.0, fe[:], ALU.min, ALU.subtract).then_inc(s["logf_done"], 1)
            dve.wait_ge(s["c_ready"], 1)
            dve.tensor_copy(ct[:], t_bank[1][0:HEADS, 0:S]).then_inc(s["ct_done"], 1)
            dve.tensor_copy(cn[:].rearrange("p a b -> p (a b)"), t_bank[0][:, 0:TOK * HEADS])\
                .then_inc(s["cn_done"], 1)
            dve.wait_ge(s["cn_done"], 1)
            attention("fox", "fox")
            chunks("w_o1", residual("w_o1"))
            norm("norm_mlp1")
            transposed("norm_mlp1", [(xt_lo, xt_hi, 6)])
            ffn("mlp1", N_MLP, MLPC, 0, 2 * S)
            add_residual("mlp1", 1.0)
            dve.wait_ge(s["row2_in"], 16)
            final("final2")

        @block.tensor
        def _(pe):
            def ready(c, i=0):
                pe.wait_ge(s["lo_ready"], RING + c + 1 + RING * i)

            def three(dst, a, b, first, last, swap=False):
                for n, (p, q) in enumerate(((a[1], b[0]), (a[0], b[0]), (a[0], b[1]))):
                    ins = pe.matmul(dst, p, q, start=first and n == 0, stop=last and n == 2)
                return ins

            def slot(c, k, w):
                return [buf[:, c % RING, 0:w].rearrange("p (k n) -> p k n", k=k) for buf in (w_hi, w_lo)]

            def part(pairs, k, cols):
                return [buf[:, k, cols] for buf in pairs]

            def tok_cols(tok):
                return slice(tok * P, (tok + 1) * P)

            def transpose_all(phase, src, wait):
                for tok in range(TOK):
                    wait(tok)
                    for k in range(KT):
                        o = (k % 2) * S + tok * P
                        ins = pe.transpose(bank[TURN_BANK[phase] + k // 2][:, o:o + P], src[:, tok, k * P:(k + 1) * P], ident[:])
                        if tok == TOK - 1 and k % 2:
                            ins.then_inc(s["tr_ready"], 1)

            def norm(phase):
                def wait(tok):
                    pe.wait_ge(s["xn_done"], at(phase, "xn_done") + tok + 1)
                transpose_all(phase, xn, wait)

            def rows_times(c, i, banks, src, first_wait):
                for j in range(4):
                    ready(c + j, i)
                    if first_wait:
                        first_wait(j)
                    w = slot(c + j, 2, 1024)
                    for k in (2 * j, 2 * j + 1):
                        for tok in range(TOK):
                            ins = three(banks[tok][:], part(src, k, tok_cols(tok)), [v[:, k % 2, :] for v in w],
                                        k == 0, k == KT - 1)
                    ins.then_inc(s["used"], 1)

            def stationary(phase, sets=1):
                return lambda j: pe.wait_ge(s["tr_lo"], at(phase, "tr_lo") + sets * (2 * j + 2))

            def ffn(phase, norm_phase, n, width, t_cols):
                b = at(phase, "units")
                tiles_in = width // P
                def up_half(c, i, m, js, first_wait=None):
                    for j in js:
                        ready(c + j, i)
                        if first_wait:
                            first_wait(j)
                        if j == 0:
                            pe.wait_ge(s["h_done"], at(phase, "h_done") + 2 * m) if first_wait is None else None
                        w = slot(c + j, 2, 1024)
                        for k in (2 * j, 2 * j + 1):
                            for tok in range(TOK):
                                ins = three(gu_bank[tok][:], part((xt_hi, xt_lo), k, tok_cols(tok)),
                                            [v[:, k % 2, :] for v in w], k == 0, k == KT - 1)
                        ins.then_inc(s["used"], 1)

                def turn(m):
                    pe.wait_ge(s["h_done"], at(phase, "h_done") + 2 * m + 2)
                    for t in range(2):
                        for q in range(tiles_in // 2):
                            for tok in range(TOK):
                                o = q * S + tok * P
                                k = t * (tiles_in // 2) + q
                                ins = pe.transpose(t_bank[t][:, o:o + P], work[1][:, tok, k * P:(k + 1) * P],
                                                   ident[:])
                        ins.then_inc(s["ht_ready"], 1)

                def down(c, i, m, last):
                    for j in range(4):
                        ready(c + j, i)
                        if j == 0:
                            pe.wait_ge(s["ht_lo"], at(phase, "ht_lo") + 2 * m + 2)
                        if tiles_in == 2:
                            w = slot(c + j, 1, 512)
                            for tok in range(TOK):
                                end = last and j >= 2
                                ins = three(bank[2 * tok + j % 2][:], part((ht_hi, ht_lo), j // 2, tok_cols(tok)),
                                            [v[:, 0, :] for v in w], False, end)
                        else:
                            w = slot(c + j, 2, 1024)
                            for tok in range(TOK):
                                for half in range(2):
                                    ins = three(bank[2 * tok + half][:], part((ht_hi, ht_lo), j, tok_cols(tok)),
                                                [v[:, half, :] for v in w], False, last and j == 3)
                        ins.then_inc(s["used"], 1)

                up_half(b, 0, 0, range(4), stationary(norm_phase))
                for q in range(4):
                    pe.matmul(bank[q][:], zeros[:, 0:P], zeros[:], start=True, stop=False)
                with pe.Fori(0, n - 1) as i:
                    up_half(b + 4, i, i + 1, (0, 1))
                    turn(i)
                    up_half(b + 4, i, i + 1, (2, 3))
                    down(b + 8, i, i, False)
                turn(n - 1)
                down(b + RING * n - 4, 0, n - 1, True)

            def attention(phase, kind, norm_phase):
                b = at(phase, "units")
                hp = at(phase, "z_ready")
                sets = 2 if kind == "fox" else 1
                xq = (xq_hi, xq_lo) if kind == "fox" else (xt_hi, xt_lo)
                xkv = (xt_hi, xt_lo)

                def project_t(c, i, dst, src, wait):
                    ready(c, i)
                    w = slot(c, KT, 1024)
                    for k in range(KT):
                        if wait and k % 2 == 0:
                            wait(k // 2)
                        ins = three(dst[:, 0:S], [v[:, k, :] for v in w], part(src, k, slice(0, S)),
                                    k == 0, k == KT - 1)
                    ins.then_inc(s["used"], 1)

                def q_part(c, i, wait=None):
                    project_t(c, i, q_bank, xq, wait)

                def k_part(c, i):
                    project_t(c + 1, i, k_bank, xkv, None)

                def v_part(c, i):
                    for j in range(2):
                        ready(c + 2 + j, i)
                        w = slot(c + 2 + j, 4, 512)
                        for k in range(4 * j, 4 * j + 4):
                            for tok in range(TOK):
                                for n, (p, q) in enumerate(((1, 0), (0, 0), (0, 1))):
                                    ins = pe.matmul(v_bank[:, tok * P:(tok + 1) * P],
                                                    xkv[p][:, k, tok_cols(tok)], w[q][:, k % 4, :],
                                                    start=k == 0 and tok == 0 and n == 0,
                                                    stop=k == KT - 1 and n == 2, skip_group_check=True)
                        ins.then_inc(s["used"], 1)

                def scores(pr, e):
                    pe.wait_ge(s["qt_done"], at(phase, "qt_done") + pr + 1)
                    pe.wait_ge(s["kt_done"], at(phase, "kt_done") + pr + 1)
                    for h in range(2):
                        rows = slice(h * DH, (h + 1) * DH)
                        q, k, z = qt[rows, e, :], kt[rows, e, :], z_bank[h]
                        if kind == "stick":
                            pe.matmul(z[:, 0:S], k[:, 0:P], q[:, 0:S], start=True, stop=True)
                            ins = pe.matmul(z[:, S:3 * P], k[:, P:S], q[:, P:S], start=False, stop=True,
                                            skip_group_check=True)
                        else:
                            pe.matmul(z[:, 0:P], q[:, 0:P], k[:, 0:P], start=True, stop=True)
                            ins = pe.matmul(z[:, P:3 * P], q[:, P:S], k[:, 0:S], start=False,
                                            stop=True, skip_group_check=True)
                            if kind == "fox":
                                c = c_row[0:1, ds((2 * pr + h) * S, S)]
                                pe.matmul(z[:, 0:P], nones[0:1, :], c_row[0:1, ds((2 * pr + h) * S, P)],
                                          start=False, stop=True, skip_group_check=True)
                                ins = pe.matmul(z[:, P:3 * P], nones[0:1, :], c, start=False, stop=True,
                                                skip_group_check=True)
                        ins.then_inc(s["z_ready"], 1)

                def middle(pr):
                    for h in range(2):
                        if kind == "stick":
                            pe.wait_ge(s["spm_done"], at(phase, "spm_done") + 2 * pr + h + 1)
                            z, sp = z_bank[h], work[1]
                            pe.matmul(z[:, 0:S], ntri[:], sp[:, h, 0:S], start=False, stop=True,
                                      skip_group_check=True)
                            pe.matmul(z[:, P:S], nones[:], sp[:, h, S:3 * P], start=False, stop=True,
                                      skip_group_check=True)
                            ins = pe.matmul(z[:, S:3 * P], ntri[:], sp[:, h, S:3 * P], start=False, stop=True,
                                            skip_group_check=True)
                        else:
                            pe.wait_ge(s["pn_done"], at(phase, "pn_done") + 2 * pr + h + 1)
                            for o in range(3):
                                ins = pe.transpose(t_bank[h][:, o * P:(o + 1) * P],
                                                   work[1][:, h, o * P:(o + 1) * P], ident[:])
                        ins.then_inc(s["r_ready"], 1)

                def weighted(pr, e):
                    pe.wait_ge(s["v_done"], at(phase, "v_done") + pr + 1)
                    for h in range(2):
                        if kind == "stick":
                            pe.wait_ge(s["wm_done"], at(phase, "wm_done") + 2 * pr + h + 1)
                        else:
                            pe.wait_ge(s["w_done"], hp + 2 * pr + h + 1)
                        rows, cols = slice(h * DH, (h + 1) * DH), slice(h * DH, (h + 1) * DH)
                        pe.matmul(y_bank[rows, 0:S], vn[:, e, 0, cols], work[2][:, h, 0:S],
                                  start=True, stop=False)
                        ins = pe.matmul(y_bank[rows, P:S], vn[:, e, 1, cols], work[2][:, h, S:3 * P],
                                        start=False, stop=True)
                    ins.then_inc(s["y_ready"], 1)

                def period(c, i, pr, e):
                    scores(pr, e)
                    q_part(c + 4, i)
                    k_part(c + 4, i)
                    middle(pr)
                    v_part(c + 4, i)
                    weighted(pr, e)

                if kind == "fox":
                    stationary(norm_phase, 2)(3)
                    pe.wait_ge(s["wf_lo_done"], 1)
                    for tok in range(TOK):
                        for k in range(KT):
                            ins = three(t_bank[0][:, tok * HEADS:(tok + 1) * HEADS],
                                        part(xkv, k, tok_cols(tok)), [v[:, k, :] for v in (wf_hi, wf_lo)],
                                        k == 0, k == KT - 1)
                    ins.then_inc(s["f_ready"], 1)
                q_part(b, 0, stationary(norm_phase, sets))
                k_part(b, 0)
                v_part(b, 0)
                if kind == "fox":
                    pe.wait_ge(s["logf_done"], 1)
                    l0, l1, ctp, cnp = logf[:, 0, :], logf[:, 1, :], t_bank[1], t_bank[0]
                    pe.matmul(ctp[0:HEADS, 0:P], l0, tri[:], start=True, stop=True)
                    pe.matmul(ctp[0:HEADS, P:S], l0, ones[:], start=True, stop=False)
                    pe.matmul(ctp[0:HEADS, P:S], l1, tri[:], start=False, stop=True)
                    pe.matmul(cnp[:, 0:HEADS], tri[:], l0, start=True, stop=True)
                    pe.matmul(cnp[:, HEADS:2 * HEADS], ones[:], l0, start=True, stop=False)
                    pe.matmul(cnp[:, HEADS:2 * HEADS], tri[:], l1, start=False, stop=True)\
                        .then_inc(s["c_ready"], 1)
                    pe.wait_ge(s["cn_done"], 1)
                    pe.wait_ge(s["c_row_in"], 16)
                with pe.Fori(0, PAIRS // 2 - 1) as i:
                    period(b, i, 2 * i, 0)
                    period(b + 4, i, 2 * i + 1, 1)
                period(b + 4 * (PAIRS - 2), 0, PAIRS - 2, 0)
                scores(PAIRS - 1, 1)
                middle(PAIRS - 1)
                weighted(PAIRS - 1, 1)

            def chunk(phase, c, i, m, e, src, first_wait=None, bank_wait=True):
                if bank_wait:
                    pe.wait_ge(s["pj_done"], at(phase, "pj_done") + 2 * m - 2)
                rows_times(c, i, bank[2 * e:2 * e + 2], src, first_wait)

            XT, YT = (xt_hi, xt_lo), (yt_hi, yt_lo)

            def chunks(phase, src, first_wait=None, bank_wait=True):
                b, n = at(phase, "units"), dict(PHASES)[phase]["units"] // RING
                if n == 1:
                    for e in range(2):
                        chunk(phase, b + 4 * e, 0, e, e, src, first_wait if e == 0 else None, False)
                else:
                    for e in range(2):
                        chunk(phase, b + 4 * e, 0, e, e, src, None, False)
                    with pe.Fori(1, n) as i:
                        for e in range(2):
                            chunk(phase, b + 4 * e, i, 2 * i + e, e, src)

            pe.sem_inc(s["used"], RING)
            pe.wait_ge(s["zero_done"], 2)
            pe.wait_ge(s["const_done"], 6)
            pe.wait_ge(s["gain_in"], 16 * 9)
            pe.transpose(bank[0][:, 0:68], gain_rows[0:68, :], ident[0:68, 0:68]).then_inc(s["gain_ready"], 1)
            pe.wait_ge(s["ws_in"], 16)
            for g in range(GROUPS):
                ins = pe.transpose(bank[1][:, g * P:(g + 1) * P], ws[:, g, :], ident[:])
            ins.then_inc(s["ws_ready"], 1)
            pe.wait_ge(s["wst_done"], 1)
            norm("norm_ff1")
            ffn("ff1", "norm_ff1", N_FF, FFC, S)
            norm("norm_mix")
            attention("stick", "stick", "norm_mix")
            pe.wait_ge(s["y_lo"], PAIRS)
            chunks("a_in", XT)
            pe.wait_ge(s["pj_done"], at("gates", "pj_done"))
            chunks("gates", XT)
            for n in range(TOK * GROUPS):
                tok, g = divmod(n, GROUPS)
                pe.wait_ge(s["v_ln"], tok + 1)
                ins = pe.matmul(bank[4 + 2 * tok + g // 2][:, (g % 2) * GD:(g % 2 + 1) * GD], wst[:, g, :],
                                a_uv[:, tok, g * GD:(g + 1) * GD], start=True, stop=True)
                if g % 2:
                    ins.then_inc(s["smix_ready"], 1)
            pe.wait_ge(s["pj_done"], at("branch_b", "pj_done"))
            b = at("branch_b", "units")
            chunk("branch_b", b, 0, 0, 0, YT, None, False)
            transpose_all("tr_a", a_uv[:, :, D:2 * D],
                          lambda tok: pe.wait_ge(s["ya_done"], TOK * GROUPS))
            chunk("branch_b", b + 4, 0, 1, 1, YT, None, False)
            pe.wait_ge(s["pj_done"], at("branch_a", "pj_done"))
            chunks("branch_a", XT, stationary("tr_a"))
            transpose_all("tr_m", xn, lambda tok: pe.wait_ge(s["m_done"], 4))
            chunks("w_out", YT, stationary("tr_m"))
            norm("norm_ff2")
            ffn("ff2", "norm_ff2", N_FF, FFC, S)
            norm("norm_moba")
            attention("moba", "moba", "norm_moba")
            pe.wait_ge(s["y_lo"], 2 * PAIRS)
            chunks("w_o0", YT)
            norm("norm_mlp0")
            ffn("mlp0", "norm_mlp0", N_MLP, MLPC, 2 * S)
            norm("norm_fox")
            attention("fox", "fox", "norm_fox")
            pe.wait_ge(s["y_lo"], 3 * PAIRS)
            chunks("w_o1", YT)
            norm("norm_mlp1")
            ffn("mlp1", "norm_mlp1", N_MLP, MLPC, 2 * S)


_INS = ["x", "ff1_norm", "ff1_w_gate", "ff1_w_up", "ff1_w_down", "mix_norm", "w_in", "b_gate", "gmlp_ln_g",
        "gmlp_ln_b", "gmlp_w_s", "gmlp_b_s", "w_branch_a", "w_branch_b", "w_out", "ff2_norm", "ff2_w_gate",
        "ff2_w_up", "ff2_w_down", "final_norm", "attn_norm_2", "moba_w_qkv_2", "fox_w_q_2", "w_o_2", "kv_norm_2",
        "w_kv_2", "w_f_2", "b_f_2", "mlp_norm_2", "w_up_2", "w_down_2", "final_norm_2"]


def kernel(**inputs):
    import concourse.bacc as _bacc
    from concourse.bass_utils import run_bass_kernel_spmd as _run

    nc = _bacc.Bacc("TRN2", target_bir_lowering=False, num_devices=1)
    arrays, args = {}, []
    for name in _INS:
        a = np.ascontiguousarray(inputs[name])
        arrays[f"in_{name}"] = a
        args.append(nc.dram_tensor(f"in_{name}", a.shape, mybir.dt.from_np(a.dtype), kind="ExternalInput").ap())
    args.append(nc.dram_tensor("out_x", (1, S, D), F32, kind="ExternalOutput").ap())
    two_blocks(nc, *args)
    return _run(nc, [arrays], core_ids=[0]).results[0]["out_x"]
```

```python
from contextlib import ExitStack

import numpy as np
import concourse.bass as bass
from concourse import mybir
from concourse.alu_op_type import AluOpType as ALU

ACT = mybir.ActivationFunctionType
F32 = mybir.dt.float32
F32R = mybir.dt.float32r
BF16 = mybir.dt.bfloat16
I32 = mybir.dt.int32
AX_X = mybir.AxisListType.X
ds = bass.ds

P = 128
D = 1024
KT = D // P
TOK = 2
S = TOK * P
HEADS = 16
DH = 64
PAIRS = HEADS // 2
FF = 2816
FFC = 256
MLPC = 512
N_FF = FF // FFC
N_MLP = 4 * D // MLPC
GROUPS = 4
GD = D // GROUPS
CHUNK = 64
EPS = 1e-6
NEG = -1e30
FAR = 1e33
RING = 8
RAW = 4
WIDE = 1024
AHEAD = 4

PROJ_SEMS = lambda chunks: {"pj_done": 2 * chunks}
TR = lambda sets: {"tr_ready": 4, "tr_hi": 8 * sets, "tr_lo": 8 * sets}
STAT = {"ms_done": 2, "rms_done": 2, "rstd_done": 2}


def ffn_sems(n):
    return {"act_done": 2 * n, "h_done": 2 * n, "ht_ready": 2 * n, "ht_hi": 2 * n, "ht_lo": 2 * n, "x_done": 4,
            "units": RING * n}


def att_sems(extra):
    return {"diag_done": 1, "rbc_ready": 1, "rbc_done": 1, "vall_done": 4, "v_done": PAIRS, "qt_done": PAIRS,
            "kt_done": PAIRS, "z_ready": HEADS, "r_ready": HEADS, "w_done": HEADS, "y_ready": PAIRS,
            "y_hi": PAIRS, "y_lo": PAIRS, "units": RING + 4 * PAIRS, **extra}


STICK = {"abs_done": HEADS, "exp_done": HEADS, "ln_done": HEADS, "sp_done": HEADS, "spm_done": HEADS,
         "wm_done": HEADS}
SOFT = {"sm_done": HEADS, "max_done": HEADS, "p_done": HEADS, "rs_done": HEADS, "pn_done": HEADS}

PHASES = [
    ("turn_ff1", TR(1)), ("stat_ff1", STAT), ("ff1", ffn_sems(N_FF)),
    ("turn_mix", TR(1)), ("stat_mix", STAT), ("stick", att_sems(STICK)),
    ("a_in", {**PROJ_SEMS(4), "units": 16}), ("gates", {**PROJ_SEMS(4), "units": 16}),
    ("branch_b", {**PROJ_SEMS(2), "units": 8}), ("turn_a", TR(1)), ("branch_a", {**PROJ_SEMS(2), "units": 8}),
    ("turn_m", TR(1)), ("w_out", {"units": 8, "x_done": 4}),
    ("turn_ff2", TR(1)), ("stat_ff2", STAT), ("ff2", ffn_sems(N_FF)),
    ("turn_moba", TR(1)), ("stat_final1", {**STAT, "x_done": 2}),
    ("stat_moba", STAT), ("moba", att_sems(SOFT)),
    ("w_o0", {"units": 8, "x_done": 4}),
    ("turn_mlp0", TR(1)), ("stat_mlp0", STAT), ("mlp0", ffn_sems(N_MLP)),
    ("turn_fox", TR(2)), ("stat_fox", STAT), ("fox", att_sems(SOFT)),
    ("w_o1", {"units": 8, "x_done": 4}),
    ("turn_mlp1", TR(1)), ("stat_mlp1", STAT), ("mlp1", ffn_sems(N_MLP)),
    ("final2", {**STAT, "x_done": 2}),
]
def begins():
    now, at = {}, {}
    for name, adds in PHASES:
        at[name] = dict(now)
        for key, n in adds.items():
            now[key] = now.get(key, 0) + n
    at["end"] = now
    return at


AT = begins()
UNITS = AT["end"]["units"]


def at(phase, key):
    return AT[phase].get(key, 0)


def unit_shapes():
    shapes = []
    for name, adds in PHASES:
        n = adds.get("units", 0)
        if name in ("ff1", "ff2"):
            shapes += [(1024, 2)] * 4
            for c in range(N_FF):
                shapes += ([(1024, 2)] * 4 if c < N_FF - 1 else []) + [(512, 1)] * 4
        elif name in ("stick", "moba", "fox"):
            shapes += [(1024, 1)] * RING + [(512, 1)] * (4 * PAIRS)
        else:
            shapes += [(1024, 1)] * n
    assert len(shapes) == UNITS
    return shapes


UNIT = unit_shapes()


def landed_value(c, i):
    def upto(u):
        return sum(16 * UNIT[v][1] for v in range(u % RAW, u + 1, RAW))
    if isinstance(i, int) and i == 0:
        return upto(c)
    return upto(c) + (upto(c + RING) - upto(c)) * i


def two_blocks(nc, x_in, ff1_norm, ff1_w_gate, ff1_w_up, ff1_w_down, mix_norm, w_in, b_gate, gmlp_ln_g,
               gmlp_ln_b, gmlp_w_s, gmlp_b_s, w_branch_a, w_branch_b, w_out, ff2_norm, ff2_w_gate, ff2_w_up,
               ff2_w_down, final_norm, attn_norm_2, moba_w_qkv_2, fox_w_q_2, w_o_2, kv_norm_2, w_kv_2, w_f_2,
               b_f_2, mlp_norm_2, w_up_2, w_down_2, final_norm_2, out):
    ctx = ExitStack()
    with ctx:
        def sb(name, shape, dt=F32, scope=ctx):
            return scope.enter_context(nc.sbuf_tensor(name, shape, dt))

        def sem(name):
            return ctx.enter_context(nc.semaphore(name))

        raw = sb("raw", [P, RAW, WIDE])
        w_hi = sb("w_hi", [P, RING, WIDE], F32R)
        w_lo = sb("w_lo", [P, RING, WIDE], F32R)
        x = sb("x", [P, TOK, D])
        side = sb("side", [P, TOK, D])
        xt_hi = sb("xt_hi", [P, KT, S], F32R)
        xt_lo = sb("xt_lo", [P, KT, S], F32R)
        yt_hi = sb("yt_hi", [P, KT, S], F32R)
        yt_lo = sb("yt_lo", [P, KT, S], F32R)
        ht_hi = sb("ht_hi", [P, 4, S], F32R)
        ht_lo = sb("ht_lo", [P, 4, S], F32R)
        work = [sb(f"work{n}", [P, 2, 512]) for n in range(3)]
        ws = side[:, 0, 0:GROUPS * P].rearrange("p (g s) -> p g s", g=GROUPS)
        qt = sb("qt", [P, 2, S])
        kt = sb("kt", [P, 2, S])
        vn = sb("vn", [P, 2, TOK, P])
        row_gain = sb("row_gain", [P, D])
        ident = sb("ident", [P, P])
        tri = sb("tri", [P, P])
        ntri = sb("ntri", [P, P])
        ones = sb("ones", [P, P])
        nones = sb("nones", [P, P])
        zeros = sb("zeros", [P, 512], BF16)
        gain_rows = sb("gain_rows", [P, P])
        gain = sb("gain", [P, 88])
        diag = work[1][:, :, 0:P]
        rbc = sb("rbc", [P, S])
        ms = sb("ms", [P, 2])
        rms = sb("rms", [P, 2])
        eps = sb("eps", [P, 1])
        sqrt_warm = sb("sqrt_warm", [P, 1])
        rstd = sb("rstd", [P, 2])
        rstd_f = sb("rstd_f", [P, 2])
        ms_half = sb("ms_half", [P, 2])
        mx = sb("mx", [P, 2, 2])
        rsum = sb("rsum", [P, 2, 2])
        rinv = sb("rinv", [P, 2, 2])
        one = ExitStack()
        a_uv = sb("a_uv", [P, TOK, 2 * D], scope=one)
        gates = sb("gates", [P, TOK, 2 * D], scope=one)
        ln_rows = sb("ln_rows", [P, 2, D], scope=one)
        wst = sb("wst", [P, GROUPS, P], scope=one)
        bn6 = sb("bn6", [P, TOK * GROUPS, 6], scope=one)
        bn2 = sb("bn2", [P, TOK * GROUPS, 2], scope=one)
        ln_rstd = sb("ln_rstd", [P, TOK * GROUPS], scope=one)
        one.close()
        two = ctx.enter_context(ExitStack())
        xq_hi = sb("xq_hi", [P, KT, S], F32R, scope=two)
        xq_lo = sb("xq_lo", [P, KT, S], F32R, scope=two)
        dist = sb("dist", [P, 3 * P], scope=two)
        dist_i = sb("dist_i", [P, 3 * P], I32, scope=two)
        mask = sb("mask", [P, 3 * P], scope=two)
        nslope = sb("nslope", [P, HEADS], scope=two)
        wf = sb("wf", [P, KT, HEADS], scope=two)
        wf_hi = sb("wf_hi", [P, KT, HEADS], F32R, scope=two)
        wf_lo = sb("wf_lo", [P, KT, HEADS], F32R, scope=two)
        bf = sb("bf", [P, HEADS], scope=two)
        fz = sb("fz", [P, TOK, HEADS], scope=two)
        fe = sb("fe", [P, TOK, HEADS], scope=two)
        logf = sb("logf", [P, TOK, HEADS], scope=two)
        cn = sb("cn", [P, TOK, HEADS], scope=two)
        ct = sb("ct", [HEADS, S], scope=two)
        c_row = sb("c_row", [1, HEADS * S], scope=two)

        bank = [ctx.enter_context(nc.psum_tensor(f"bank{n}", [P, 512], F32)) for n in range(8)]
        gu_bank, t_bank = bank[4:6], bank[6:8]
        q_bank, k_bank, y_bank, rbc_bank = bank[0], bank[1], bank[3], bank[4]

        landed = [sem(f"landed{n}") for n in range(RAW)]
        s = {name: sem(name) for name in (
            "hi_ready", "lo_ready", "used",
            "x_in", "rows_in", "gain_in", "gain_ready", "gain_cols", "gain_prod", "gain_in2", "blk1_in", "ws_ready", "wst_done",
            "ws_in", "pool_turns", "sp_turns", "const_done", "const2_done", "gate_in", "wf_in", "row2_in", "zero_done",
            "ms_done", "rms_done", "rstd_done", "rprod_done", "half_done", "diag_done", "rbc_ready", "rbc_done", "vall_done", "tr_ready", "tr_hi", "tr_lo",
            "act_done", "h_done", "ht_ready", "ht_hi", "ht_lo", "x_done",
            "qt_done", "kt_done", "v_done", "z_ready", "r_ready",
            "abs_done", "exp_done", "ln_done", "sp_done", "spm_done", "w_done", "wm_done",
            "y_ready", "y_hi", "y_lo", "sm_done", "max_done", "p_done", "rs_done", "pn_done",
            "pj_done", "gelu_done", "gate_done", "bn_done", "bna_done", "lns_done", "lnr_done", "ln_done2",
            "lng_done", "v_ln", "smix_ready", "ya_done", "prod_done", "m_done",
            "wf_hi_done", "wf_lo_done", "f_ready", "fz_done", "fabs_done", "fexp_done", "fln_done", "logf_done",
            "c_ready", "ct_done", "cn_done", "c_row_in", "stored")}

        def tiles(w):
            return w.rearrange("(k p) n -> p k n", p=P)

        win, wba, wbb, wout = (tiles(w[0]) for w in (w_in, w_branch_a, w_branch_b, w_out))
        qkv_moba = [tiles(moba_w_qkv_2[0])[:, :, n * D:(n + 1) * D] for n in range(3)]
        kv = tiles(w_kv_2)
        qkv_fox = [tiles(fox_w_q_2[0]), kv[:, :, 0:D], kv[:, :, D:2 * D]]
        qkv_stick = [win[:, :, (2 + n) * D:(3 + n) * D] for n in range(3)]
        wo = [tiles(w_o_2[n]) for n in range(2)]

        def ht_of(buf, t, t_cols):
            if t_cols == S:
                return buf[:, t, :]
            return buf[:, 2 * t:2 * t + 2, :].rearrange("p a b -> p (a b)")

        def consumed(eng, c, i=0):
            eng.wait_ge(s["used"], RING + c + 1 + RING * i)

        block = ctx.enter_context(nc.Block())

        @block.sync
        def _(sp):
            def room(c, i):
                sp.wait_ge(s["lo_ready"], RING + c - RAW + 1 + RING * i)

            def send(c, i, dst, src):
                sp.dma_start(dst, src).then_inc(landed[c % RAW], 16)

            def slot(c, k, w):
                return raw[:, c % RAW, 0:w].rearrange("p (k n) -> p k n", k=k)

            def small_loads():
                rows = [mix_norm[0:1], ff2_norm[0:1], attn_norm_2[0:1], attn_norm_2[1:2],
                        mlp_norm_2[0:1], mlp_norm_2[1:2], kv_norm_2.rearrange("(a n) -> a n", a=1)]
                for n, g in enumerate(rows):
                    sp.dma_start(gain_rows[8 * n + 8:8 * n + 16, :], g.rearrange("a (k p) -> (a k) p", p=P))\
                        .then_inc(s["rows_in"], 16)
                sp.dma_start(gain_rows[64:68, :], gmlp_b_s[0]).then_inc(s["rows_in"], 16)
                sp.dma_start(gain_rows[68:76, :], final_norm.rearrange("(k p) -> k p", p=P))\
                    .then_inc(s["rows_in"], 16)
                sp.dma_start(ws, gmlp_w_s[0].rearrange("g t s -> t g s")).then_inc(s["ws_in"], 16)

            def ff_units(phase, w_gate, w_up, w_down, after_first=None):
                b = at(phase, "units")
                wg, wu, wd = tiles(w_gate[0]), tiles(w_up[0]), tiles(w_down[0])

                def gate_up(c, i, chunk):
                    for j in range(4):
                        room(c + j, i)
                        for half, w in enumerate((wg, wu)):
                            send(c + j, i, slot(c + j, 2, 1024)[:, :, half * FFC:(half + 1) * FFC],
                                 w[:, 2 * j:2 * j + 2, ds(chunk * FFC, FFC)])

                def down(c, i, chunk):
                    for j in range(4):
                        room(c + j, i)
                        send(c + j, i, slot(c + j, 1, 512),
                             wd[:, ds(2 * chunk + j % 2, 1), (j // 2) * 512:(j // 2) * 512 + 512])

                gate_up(b, 0, 0)
                if after_first:
                    after_first()
                with sp.Fori(0, N_FF - 1) as i:
                    gate_up(b + 4, i, i + 1)
                    down(b + 8, i, i)
                down(b + RING * N_FF - 4, 0, N_FF - 1)

            def mlp_units(phase, w_up, w_down):
                b = at(phase, "units")
                wu, wd = tiles(w_up), tiles(w_down)

                def up(c, i, chunk):
                    for j in range(4):
                        room(c + j, i)
                        send(c + j, i, slot(c + j, 2, 1024), wu[:, 2 * j:2 * j + 2, ds(chunk * MLPC, MLPC)])

                def down(c, i, chunk):
                    for j in range(4):
                        room(c + j, i)
                        send(c + j, i, slot(c + j, 2, 1024),
                             wd[:, ds(4 * chunk + 2 * (j % 2), 2), (j // 2) * 512:(j // 2) * 512 + 512])

                up(b, 0, 0)
                with sp.Fori(0, N_MLP - 1) as i:
                    up(b + 4, i, i + 1)
                    down(b + 8, i, i)
                down(b + RING * N_MLP - 4, 0, N_MLP - 1)

            def att_units(phase, q_w, k_w, v_w):
                b = at(phase, "units")

                def pair(c, i, pr):
                    for n, w in enumerate((q_w, k_w)):
                        for j in range(2):
                            u = c + 2 * n + j
                            room(u, i)
                            send(u, i, slot(u, 4, 512), w[:, 4 * j:4 * j + 4, ds(pr * P, P)])

                for u in range(RING):
                    room(b + u, 0)
                    e, j = divmod(u, 4)
                    send(b + u, 0, slot(b + u, 2, 1024), v_w[:, 2 * j:2 * j + 2, e * 512:(e + 1) * 512])
                with sp.Fori(0, PAIRS // 2) as i:
                    pair(b + RING, i, 2 * i)
                    pair(b + RING + 4, i, 2 * i + 1)

            def proj_units(phase, w, col):
                b, n = at(phase, "units"), dict(PHASES)[phase]["units"] // RING

                def body(i, first):
                    for e in range(2):
                        for j in range(4):
                            c = b + 4 * e + j
                            room(c, i)
                            if n > 1 and e == 0 and j == 0:
                                sp.sem_inc(s["sp_turns"], 1)
                            send(c, i, slot(c, 2, 1024), w[:, 2 * j:2 * j + 2, ds(first + 512 * e, 512)])
                if n == 1:
                    body(0, 0)
                else:
                    with sp.Fori(0, n) as i:
                        body(i, sp.snap(col(i)))

            ff_units("ff1", ff1_w_gate, ff1_w_up, ff1_w_down, small_loads)
            att_units("stick", *qkv_stick)
            proj_units("a_in", win, lambda i: D - D * i)
            proj_units("gates", win, lambda i: 5 * D + D * i)
            proj_units("branch_b", wbb, lambda i: 0)
            proj_units("branch_a", wba, lambda i: 0)
            proj_units("w_out", wout, lambda i: 0)
            ff_units("ff2", ff2_w_gate, ff2_w_up, ff2_w_down)
            att_units("moba", *qkv_moba)
            proj_units("w_o0", wo[0], lambda i: 0)
            mlp_units("mlp0", w_up_2[0], w_down_2[0])
            att_units("fox", *qkv_fox)
            proj_units("w_o1", wo[1], lambda i: 0)
            mlp_units("mlp1", w_up_2[1], w_down_2[1])
            for tok in range(TOK):
                sp.wait_ge(s["x_done"], at("final2", "x_done") + tok + 1)
                sp.dma_start(out[0, tok * P:(tok + 1) * P, :], x[:, tok, :]).then_inc(s["stored"], 16)
            sp.wait_ge(s["stored"], 16 * TOK)

        @block.gpsimd
        def _(pool):
            count = {"n": 0}

            def const(ins, name="const_done"):
                ins.then_inc(s[name], 1)
                count["n"] += 1
                pool.wait_ge(s[name], count["n"])

            pool.memset(zeros[:], 0.0).then_inc(s["zero_done"], 1)
            pool.memset(eps[:], EPS).then_inc(s["zero_done"], 1)
            const(pool.memset(ident[:], 0.0))
            const(pool.affine_select(out=ident[:], in_=ident[:], compare_op=ALU.not_equal, fill=1.0, base=0,
                                     pattern=[[-1, P]], channel_multiplier=1))
            const(pool.memset(ones[:], 1.0))
            const(pool.memset(nones[:], -1.0))
            const(pool.affine_select(out=tri[:], in_=ones[:], compare_op=ALU.is_ge, fill=0.0, base=0,
                                     pattern=[[1, P]], channel_multiplier=-1))
            const(pool.affine_select(out=ntri[:], in_=nones[:], compare_op=ALU.is_ge, fill=0.0, base=0,
                                     pattern=[[-1, P]], channel_multiplier=1))
            consumed(pool, 3)
            pool.dma_start(ln_rows[:, 0, :], gmlp_ln_g.rearrange("a g c -> a (g c)").broadcast_to([P, D]))\
                .then_inc(s["blk1_in"], 16)
            pool.dma_start(ln_rows[:, 1, :], gmlp_ln_b.rearrange("a g c -> a (g c)").broadcast_to([P, D]))\
                .then_inc(s["blk1_in"], 16)
            for tok in range(TOK):
                pool.dma_start(gates[:, tok, :], b_gate.broadcast_to([P, 2 * D])).then_inc(s["gate_in"], 16)
            pool.dma_start(row_gain[:], final_norm.rearrange("(a n) -> a n", a=1).broadcast_to([P, D]))\
                .then_inc(s["gain_in2"], 16)

            def causal(buf, h):
                v = buf[:, h, 0:512].rearrange("p (b t) -> p b t", b=2)[:, :, 0:P]
                return pool.affine_select(out=v, in_=v, compare_op=ALU.is_gt, fill=0.0, base=0,
                                          pattern=[[0, 2], [1, P]], channel_multiplier=-1)

            def pair(phase, pr, e, old):
                own = at(phase, "y_ready")
                if old:
                    pool.wait_ge(s["y_ready"], own + pr - 1)
                    pool.sem_inc(s["pool_turns"], 1)
                else:
                    pool.wait_ge(s["y_ready"], own)
                    pool.wait_ge(s["vall_done"], at(phase, "vall_done") + 4)
                pool.tensor_copy(vn[:, e, :, :], side[:, :, ds(pr * P, P)]).then_inc(s["v_done"], 1)
                if phase != "stick":
                    return
                for h in range(2):
                    pool.wait_ge(s["sp_done"], 2 * pr + h + 1)
                    pool.sem_inc(s["pool_turns"], 1)
                    causal(work[1], h).then_inc(s["spm_done"], 1)
                for h in range(2):
                    pool.wait_ge(s["w_done"], 2 * pr + h + 1)
                    pool.sem_inc(s["pool_turns"], 1)
                    causal(work[2], h).then_inc(s["wm_done"], 1)

            def pairs(phase):
                for e in range(2):
                    pair(phase, e, e, False)
                with pool.Fori(1, PAIRS // 2) as i:
                    for e in range(2):
                        pair(phase, 2 * i + e, e, True)

            pairs("stick")

            pool.wait_ge(s["blk1_in"], 32)
            for tok in range(TOK):
                v = a_uv[:, tok, 0:D]
                pool.wait_ge(s["ln_done2"], GROUPS * (tok + 1))
                pool.tensor_tensor(v, v, ln_rows[:, 0, :], ALU.mult).then_inc(s["lng_done"], 1)
                pool.wait_ge(s["lng_done"], tok + 1)
                pool.tensor_tensor(v, v, ln_rows[:, 1, :], ALU.add).then_inc(s["v_ln"], 1)

            pool.wait_ge(s["x_done"], at("turn_ff2", "x_done"))
            count["n"] = 0
            for t, base in ((0, 0), (P, P)):
                const(pool.iota(dist_i[:, t:t + P + base], pattern=[[-1, P + base]], base=base,
                                channel_multiplier=1), "const2_done")
            const(pool.tensor_copy(dist[:], dist_i[:]), "const2_done")
            const(pool.memset(mask[:], 0.0), "const2_done")
            for t, base in ((0, 0), (P, P)):
                for buf, fill in ((dist, FAR), (mask, NEG)):
                    v = buf[:, t:t + P + base]
                    const(pool.affine_select(out=v, in_=v, compare_op=ALU.is_ge, fill=fill, base=base,
                                             pattern=[[-1, P + base]], channel_multiplier=1), "const2_done")
            for h in range(HEADS):
                const(pool.memset(nslope[:, h:h + 1], -float(np.float32(2.0 ** (-8.0 * (h + 1) / HEADS)))),
                      "const2_done")
            pool.dma_start(wf[:], tiles(w_f_2)).then_inc(s["wf_in"], 16)
            pool.dma_start(bf[:], b_f_2.rearrange("(a n) -> a n", a=1).broadcast_to([P, HEADS]))\
                .then_inc(s["wf_in"], 16)
            pool.wait_ge(s["x_done"], at("stat_moba", "x_done"))
            pool.dma_start(row_gain[:], final_norm_2.rearrange("(a n) -> a n", a=1).broadcast_to([P, D]))\
                .then_inc(s["row2_in"], 16)
            pairs("moba")
            pool.wait_ge(s["ct_done"], 1)
            pool.dma_start(c_row[:].rearrange("a (h t) -> a h t", h=HEADS), ct[:]).then_inc(s["c_row_in"], 16)
            pairs("fox")

        @block.scalar
        def _(act):
            act.dma_start(gain_rows[0:8, :], ff1_norm.rearrange("a (k p) -> (a k) p", p=P))\
                .then_inc(s["gain_in"], 16)
            for tok in range(TOK):
                act.dma_start(x[:, tok, :], x_in[0, tok * P:(tok + 1) * P, :]).then_inc(s["x_in"], 16)

            def hi(c, i=0):
                if c >= UNITS:
                    return
                w = UNIT[c][0]
                act.wait_ge(landed[c % RAW], landed_value(c, i))
                act.wait_ge(s["used"], c + 1 + RING * i)
                act.activation(w_hi[:, c % RING, 0:w], raw[:, c % RAW, 0:w], ACT.Copy).then_inc(s["hi_ready"], 1)

            def stat(phase, ready=None):
                act.preload_act_table_set("sqrt_and_others")
                for tok in range(TOK):
                    if ready is None:
                        act.wait_ge(s["x_done"], at(phase, "x_done"))
                    elif tok == 0:
                        ready()
                    act.activation(work[2][:].rearrange("p a b -> p (a b)"), x[:, tok, :], ACT.Square,
                                   scale=1.0 / 32.0, accum_out=ms[:, tok:tok + 1]).then_inc(s["ms_done"], 1)
                    act.wait_ge(s["ms_done"], at(phase, "ms_done") + tok + 1)
                    act.activation(rms[:, tok:tok + 1], ms[:, tok:tok + 1], ACT.Sqrt, bias=eps[:])\
                        .then_inc(s["rms_done"], 1)

            def turned(phase, half, sets):
                for b in range(2):
                    act.wait_ge(s["tr_ready"], at(phase, "tr_ready") + 2 * half + b + 1)
                    for k in range(4 * half + 2 * b, 4 * half + 2 * b + 2):
                        for dst, g in sets:
                            src = t_bank[b][:, (k % 2) * S:(k % 2 + 1) * S]
                            scale = 1.0 if g is None else gain[:, 8 * g + k:8 * g + k + 1]
                            act.activation(dst[:, k, :], src, ACT.Copy, scale=scale).then_inc(s["tr_hi"], 1)

            def ffn(phase, n, func, width, t_cols, stats):
                b = at(phase, "units")

                def chunk(c, i, m, last_up, before=lambda: None):
                    hi(c + 4, i)
                    hi(c + 5, i)
                    before()
                    for tok in range(TOK):
                        consumed(act, last_up, i)
                        act.activation(work[0][:, tok, 0:width], gu_bank[tok][:, 0:width], func,
                                       scale=rstd[:, tok:tok + 1])\
                            .then_inc(s["act_done"], 1)
                    for u in range(6, 10):
                        hi(c + u, i)
                    for t in range(2):
                        act.wait_ge(s["ht_ready"], at(phase, "ht_ready") + 2 * m + t + 1)
                        act.activation(ht_of(ht_hi, t, t_cols), t_bank[t][:, 0:t_cols], ACT.Copy)\
                            .then_inc(s["ht_hi"], 1)
                    hi(c + 10, i)
                    hi(c + 11, i)

                def rows():
                    stats()
                    act.wait_ge(s["rstd_done"], at(phase, "rstd_done"))

                chunk(b, 0, 0, b + 3, rows)
                with act.Fori(1, n - 1) as i:
                    chunk(b, i, i, b - 1)
                chunk(b + RING * (n - 1), 0, n - 1, b + RING * (n - 1) - 1)

            def attention(phase, soft, turn_b, stats):
                b = at(phase, "units")
                hp = at(phase, "z_ready")
                own = at(phase, "sm_done" if soft else "abs_done")

                def values(e):
                    consumed(act, b + 4 * e + 3)
                    for tok in range(TOK):
                        act.activation(side[:, tok, e * 512:(e + 1) * 512], bank[2 * e + tok][:], ACT.Copy,
                                       scale=rstd[:, tok:tok + 1]).then_inc(s["vall_done"], 1)

                def first_part(pr, e):
                    for h in range(2):
                        if soft:
                            act.wait_ge(s["max_done"], own + 2 * pr + h + 1)
                            for t, cols in ((0, slice(0, P)), (1, slice(P, 3 * P))):
                                ins = act.activation(work[1][:, h, cols], work[0][:, h, cols], ACT.Exp,
                                                     bias=mx[:, h, t:t + 1], accum_out=rsum[:, h, t:t + 1])
                            ins.then_inc(s["p_done"], 1)
                        else:
                            act.wait_ge(s["z_ready"], hp + 2 * pr + h + 1)
                            act.activation(work[0][:, h, 0:3 * P], bank[4 + 2 * e + h][:, 0:3 * P], ACT.Abs)\
                                .then_inc(s["abs_done"], 1)
                    if not soft:
                        for h in range(2):
                            act.wait_ge(s["abs_done"], own + 2 * pr + h + 1)
                            act.activation(work[0][:, h, 0:3 * P], work[0][:, h, 0:3 * P], ACT.Exp, scale=-1.0)\
                                .then_inc(s["exp_done"], 1)
                        for h in range(2):
                            act.wait_ge(s["exp_done"], own + 2 * pr + h + 1)
                            act.activation(work[0][:, h, 0:3 * P], work[0][:, h, 0:3 * P], ACT.Ln, bias=1.0)\
                                .then_inc(s["ln_done"], 1)

                def second_part(pr, e):
                    for h in range(2):
                        act.wait_ge(s["r_ready"], hp + 2 * pr + h + 1)
                        src = t_bank[h] if soft else bank[4 + 2 * e + h]
                        act.activation(work[2][:, h, 0:3 * P], src[:, 0:3 * P], ACT.Copy if soft else ACT.Exp)\
                            .then_inc(s["w_done"], 1)

                def y_part(pr):
                    act.wait_ge(s["y_ready"], at(phase, "y_ready") + pr + 1)
                    act.activation(yt_hi[:, ds(pr, 1), :], y_bank[:, 0:S], ACT.Copy).then_inc(s["y_hi"], 1)

                def cycle(c, i, pr, e):
                    hi(c, i)
                    hi(c + 1, i)
                    second_part(pr, e)
                    hi(c + 2, i)
                    first_part(pr + 1, 1 - e)
                    hi(c + 3, i)
                    y_part(pr)

                hi(b + 4)
                turn_b()
                hi(b + 5)
                stats()
                act.wait_ge(s["rstd_done"], at(phase, "rstd_done"))
                act.preload_act_table_set("natural_log_exp_and_others")
                hi(b + 6)
                hi(b + 7)
                if phase == "moba":
                    act.wait_ge(s["rprod_done"], 1)
                values(0)
                for u in range(8, 12):
                    hi(b + u)
                values(1)
                act.wait_ge(s["rbc_ready"], at(phase, "rbc_ready") + 1)
                act.activation(rbc[:], rbc_bank[:, 0:S], ACT.Copy).then_inc(s["rbc_done"], 1)
                hi(b + 12)
                hi(b + 13)
                if phase == "fox":
                    act.wait_ge(s["fz_done"], 1)
                    act.activation(fe[:], fz[:], ACT.Abs).then_inc(s["fabs_done"], 1)
                    act.wait_ge(s["fabs_done"], 1)
                    act.activation(fe[:], fe[:], ACT.Exp, scale=-1.0).then_inc(s["fexp_done"], 1)
                    act.wait_ge(s["fexp_done"], 1)
                    act.activation(fe[:], fe[:], ACT.Ln, bias=1.0).then_inc(s["fln_done"], 1)
                hi(b + 14)
                hi(b + 15)
                first_part(0, 0)
                with act.Fori(0, PAIRS // 2 - 1) as i:
                    cycle(b + 16, i, 2 * i, 0)
                    cycle(b + 20, i, 2 * i + 1, 1)
                cycle(b + 40, 0, PAIRS - 2, 0)
                second_part(PAIRS - 1, 1)
                y_part(PAIRS - 1)

            def chunks(phase, evac=None):
                b, n = at(phase, "units"), dict(PHASES)[phase]["units"] // RING

                def body(i):
                    for e in range(2):
                        for j in range(4):
                            hi(b + 4 * e + AHEAD + j, i)
                        if evac:
                            evac(2 * i + e, e, b + 4 * e + 3, i)
                if n == 1:
                    body(0)
                else:
                    with act.Fori(0, n - 1) as i:
                        body(i)
                    b += RING * (n - 1)
                    for e in range(2):
                        for j in range(4):
                            hi(b + 4 * e + AHEAD + j)
                        if evac:
                            evac(2 * (n - 1) + e, e, b + 4 * e + 3, 0)

            def gelu(m, e, c, i):
                for tok in range(TOK):
                    consumed(act, c, i)
                    act.activation(a_uv[:, tok, ds(m * 512, 512)], bank[2 * e + tok][:], ACT.Gelu,
                                   scale=rstd[:, tok:tok + 1])\
                        .then_inc(s["pj_done"], 1)

            def sigmoid(m, e, c, i):
                for tok in range(TOK):
                    act.wait_ge(s["pj_done"], at("gates", "pj_done") + 2 * m + tok + 1)
                    g = gates[:, tok, ds(m * 512, 512)]
                    act.activation(g, g, ACT.Sigmoid).then_inc(s["gate_done"], 1)

            def w_o(phase, sets, next_turn):
                b = at(phase, "units")
                for u in range(AHEAD, AHEAD + 6):
                    hi(b + u)
                turned(next_turn, 0, sets)
                hi(b + 10)
                hi(b + 11)

            act.wait_ge(s["gain_cols"], 1)
            turned("turn_ff1", 0, [(xt_hi, 0)])
            hi(0)
            turned("turn_ff1", 1, [(xt_hi, 0)])
            for u in range(1, AHEAD):
                hi(u)
            act.wait_ge(s["zero_done"], 2)
            ffn("ff1", N_FF, ACT.Silu, FFC, S, lambda: stat("stat_ff1", lambda: act.wait_ge(s["x_in"], 32)))
            act.wait_ge(s["gain_cols"], 2)
            turned("turn_mix", 0, [(xt_hi, 1)])
            attention("stick", False, lambda: turned("turn_mix", 1, [(xt_hi, 1)]), lambda: stat("stat_mix"))
            chunks("a_in", gelu)
            act.wait_ge(s["bna_done"], TOK * GROUPS)
            act.activation(ln_rstd[:], bn2[:, :, 1], ACT.Sqrt, bias=eps[:]).then_inc(s["lns_done"], 1)
            chunks("gates", sigmoid)
            b = at("branch_b", "units")
            for u in range(AHEAD, AHEAD + 4):
                hi(b + u)
            turned("turn_a", 0, [(xt_hi, None)])
            turned("turn_a", 1, [(xt_hi, None)])
            for u in range(AHEAD + 4, AHEAD + 8):
                hi(b + u)
            w_o("branch_a", [(yt_hi, None)], "turn_m")
            b = at("w_out", "units")
            hi(b + 4)
            turned("turn_m", 1, [(yt_hi, None)])
            for u in range(5, 10):
                hi(b + u)
            turned("turn_ff2", 0, [(xt_hi, 2)])
            hi(b + 10)
            hi(b + 11)
            turned("turn_ff2", 1, [(xt_hi, 2)])
            ffn("ff2", N_FF, ACT.Silu, FFC, S, lambda: stat("stat_ff2"))
            act.wait_ge(s["gain_prod"], 1)
            turned("turn_moba", 0, [(xt_hi, 10)])

            def two_stats():
                stat("stat_final1")
                stat("stat_moba")

            attention("moba", True, lambda: turned("turn_moba", 1, [(xt_hi, 10)]), two_stats)
            w_o("w_o0", [(xt_hi, 5)], "turn_mlp0")
            turned("turn_mlp0", 1, [(xt_hi, 5)])
            ffn("mlp0", N_MLP, ACT.Relu, MLPC, 2 * S, lambda: stat("stat_mlp0"))
            fox_sets = [(xt_hi, 7), (xq_hi, 4)]
            turned("turn_fox", 0, fox_sets)
            act.wait_ge(s["wf_in"], 32)
            act.activation(wf_hi[:], wf[:], ACT.Copy).then_inc(s["wf_hi_done"], 1)
            attention("fox", True, lambda: turned("turn_fox", 1, fox_sets), lambda: stat("stat_fox"))
            w_o("w_o1", [(xt_hi, 6)], "turn_mlp1")
            turned("turn_mlp1", 1, [(xt_hi, 6)])
            ffn("mlp1", N_MLP, ACT.Relu, MLPC, 2 * S, lambda: stat("stat_mlp1"))
            act.preload_act_table_set("sqrt_and_others")
            for half in range(2):
                for tok in range(TOK):
                    act.wait_ge(s["x_done"], at("mlp1", "x_done") + 2 * half + tok + 1)
                    dst = (ms_half if half == 0 else ms)[:, tok:tok + 1]
                    act.activation(work[2][:, tok, :], x[:, tok, half * 512:(half + 1) * 512], ACT.Square,
                                   scale=1.0 / 32.0, accum_out=dst)\
                        .then_inc(s["half_done" if half == 0 else "ms_done"], 1)
                    if half == 0:
                        act.wait_ge(s["half_done"], 2 * tok + 1)
                        act.activation(ms_half[:, tok:tok + 1], ms_half[:, tok:tok + 1], ACT.Identity, bias=eps[:])\
                            .then_inc(s["half_done"], 1)
                    else:
                        act.wait_ge(s["half_done"], 4)
                        act.wait_ge(s["ms_done"], at("final2", "ms_done") + tok + 1)
                        act.activation(rms[:, tok:tok + 1], ms[:, tok:tok + 1], ACT.Sqrt,
                                       bias=ms_half[:, tok:tok + 1]).then_inc(s["rms_done"], 1)

        @block.vector
        def _(dve):
            def lo(c, i=0):
                if c >= UNITS:
                    return
                w = UNIT[c][0]
                dve.wait_ge(s["hi_ready"], c + 1 + RING * i)
                dve.tensor_tensor(w_lo[:, c % RING, 0:w], raw[:, c % RAW, 0:w],
                                  w_hi[:, c % RING, 0:w].bitcast(F32), ALU.subtract).then_inc(s["lo_ready"], 1)

            def root(phase, dst=rstd):
                for tok in range(TOK):
                    dve.wait_ge(s["rms_done"], at(phase, "rms_done") + tok + 1)
                    dve.reciprocal(dst[:, tok:tok + 1], rms[:, tok:tok + 1]).then_inc(s["rstd_done"], 1)

            def final(phase):
                for tok in range(TOK):
                    dve.wait_ge(s["rms_done"], at(phase, "rms_done") + tok + 1)
                    dve.reciprocal(rstd_f[:, tok:tok + 1], rms[:, tok:tok + 1]).then_inc(s["rstd_done"], 1)
                    dve.wait_ge(s["rstd_done"], at(phase, "rstd_done") + tok + 1)
                    dve.scalar_tensor_tensor(x[:, tok, :], x[:, tok, :], rstd_f[:, tok:tok + 1], row_gain[:],
                                             ALU.mult, ALU.mult).then_inc(s["x_done"], 1)

            def turned(phase, half, sets):
                for b in range(2):
                    dve.wait_ge(s["tr_hi"], at(phase, "tr_hi") + len(sets) * (4 * half + 2 * b + 2))
                    for k in range(4 * half + 2 * b, 4 * half + 2 * b + 2):
                        for low, high, g in sets:
                            src = t_bank[b][:, (k % 2) * S:(k % 2 + 1) * S]
                            if g is None:
                                dve.tensor_tensor(low[:, k, :], src, high[:, k, :].bitcast(F32), ALU.subtract)\
                                    .then_inc(s["tr_lo"], 1)
                            else:
                                dve.scalar_tensor_tensor(low[:, k, :], src, gain[:, 8 * g + k:8 * g + k + 1],
                                                         high[:, k, :].bitcast(F32), ALU.mult, ALU.subtract)\
                                    .then_inc(s["tr_lo"], 1)

            def ffn(phase, n, width, off, t_cols, stats):
                b = at(phase, "units")

                def chunk(c, i, m, before=lambda: None):
                    lo(c + 4, i)
                    lo(c + 5, i)
                    before()
                    for tok in range(TOK):
                        dve.wait_ge(s["act_done"], at(phase, "act_done") + 2 * m + tok + 1)
                        if off:
                            dve.scalar_tensor_tensor(work[1][:, tok, 0:width], gu_bank[tok][:, off:off + width],
                                                     rstd[:, tok:tok + 1], work[0][:, tok, 0:width],
                                                     ALU.mult, ALU.mult).then_inc(s["h_done"], 1)
                        else:
                            dve.tensor_tensor(work[1][:, tok, 0:width], work[0][:, tok, 0:width],
                                              work[0][:, tok, 0:width], ALU.mult).then_inc(s["h_done"], 1)
                    for u in range(6, 10):
                        lo(c + u, i)
                    for t in range(2):
                        dve.wait_ge(s["ht_hi"], at(phase, "ht_hi") + 2 * m + t + 1)
                        dve.tensor_tensor(ht_of(ht_lo, t, t_cols), t_bank[t][:, 0:t_cols],
                                          ht_of(ht_hi, t, t_cols).bitcast(F32), ALU.subtract)\
                            .then_inc(s["ht_lo"], 1)
                    lo(c + 10, i)
                    lo(c + 11, i)

                chunk(b, 0, 0, stats)
                with dve.Fori(1, n - 1) as i:
                    chunk(b, i, i)
                chunk(b + RING * (n - 1), 0, n - 1)

            def add_half(phase, scale, half, last_unit):
                consumed(dve, last_unit)
                for tok in range(TOK):
                    v = x[:, tok, half * 512:(half + 1) * 512]
                    dve.scalar_tensor_tensor(v, bank[2 * half + tok][:], scale, v, ALU.mult, ALU.add)\
                        .then_inc(s["x_done"], 1)

            def ffn_end(phase, scale, between):
                b = at(phase, "units") + dict(PHASES)[phase]["units"]
                add_half(phase, scale, 0, b - 3)
                between()
                add_half(phase, scale, 1, b - 1)

            def attention(phase, kind, turn_b, stats):
                b = at(phase, "units")
                hp = at(phase, "z_ready")
                own = at(phase, "abs_done" if kind == "stick" else "sm_done")

                def q_evac(c, i, e):
                    consumed(dve, c + 1, i)
                    dve.scalar_tensor_tensor(qt[:, e, :], q_bank[:, 0:S], float(DH) ** -0.5, rbc[:],
                                             ALU.mult, ALU.mult).then_inc(s["qt_done"], 1)

                def k_evac(c, i, e):
                    consumed(dve, c + 3, i)
                    dve.tensor_tensor(kt[:, e, :], k_bank[:, 0:S], rbc[:], ALU.mult).then_inc(s["kt_done"], 1)

                def first_part(pr):
                    if kind == "stick":
                        return
                    for h in range(2):
                        dve.wait_ge(s["z_ready"], hp + 2 * pr + h + 1)
                        a, z = work[0][:, h, 0:3 * P], bank[4 + h][:, 0:3 * P]
                        if kind == "moba":
                            dve.scalar_tensor_tensor(a, dist[:], nslope[:, ds(2 * pr + h, 1)], z,
                                                     ALU.mult, ALU.add).then_inc(s["sm_done"], 1)
                        else:
                            dve.scalar_tensor_tensor(a[:, 0:P], z[:, 0:P], cn[:, 0, ds(2 * pr + h, 1)],
                                                     mask[:, 0:P], ALU.add, ALU.add)
                            dve.scalar_tensor_tensor(a[:, P:3 * P], z[:, P:3 * P], cn[:, 1, ds(2 * pr + h, 1)],
                                                     mask[:, P:3 * P], ALU.add, ALU.add)\
                                .then_inc(s["sm_done"], 1)
                    for h in range(2):
                        dve.wait_ge(s["sm_done"], own + 2 * pr + h + 1)
                        dve.tensor_reduce(mx[:, h, 0:1], work[0][:, h, 0:P], AX_X, ALU.max, negate=True)
                        dve.tensor_reduce(mx[:, h, 1:2], work[0][:, h, P:3 * P], AX_X, ALU.max, negate=True)\
                            .then_inc(s["max_done"], 1)

                def second_part(pr, e):
                    for h in range(2):
                        if kind == "stick":
                            dve.wait_ge(s["ln_done"], own + 2 * pr + h + 1)
                            dve.scalar_tensor_tensor(work[1][:, h, 0:3 * P], bank[4 + 2 * e + h][:, 0:3 * P], 0.0,
                                                     work[0][:, h, 0:3 * P], ALU.max, ALU.add)\
                                .then_inc(s["sp_done"], 1)
                        else:
                            dve.wait_ge(s["p_done"], own + 2 * pr + h + 1)
                            dve.reciprocal(rinv[:, h, :], rsum[:, h, :]).then_inc(s["rs_done"], 1)
                            dve.wait_ge(s["rs_done"], own + 2 * pr + h + 1)
                            for t, cols in ((0, slice(0, P)), (1, slice(P, 3 * P))):
                                v = work[1][:, h, cols]
                                ins = dve.tensor_scalar(v, v, rinv[:, h, t:t + 1], None, ALU.mult)
                            ins.then_inc(s["pn_done"], 1)

                def y_part(pr):
                    dve.wait_ge(s["y_hi"], at(phase, "y_hi") + pr + 1)
                    dve.tensor_tensor(yt_lo[:, ds(pr, 1), :], y_bank[:, 0:S],
                                      yt_hi[:, ds(pr, 1), :].bitcast(F32), ALU.subtract).then_inc(s["y_lo"], 1)

                def cycle(c, i, pr, e, project=True):
                    for u in range(3):
                        lo(c + u, i)
                    first_part(pr + 1)
                    lo(c + 3, i)
                    second_part(pr + 1, 1 - e)
                    y_part(pr)
                    if project:
                        q_evac(c, i, e)
                        k_evac(c, i, e)

                lo(b + 4)
                turn_b()
                lo(b + 5)
                stats()
                dve.wait_ge(s["rstd_done"], at(phase, "rstd_done"))
                if phase == "moba":
                    dve.wait_ge(s["rprod_done"], 1)
                for tok in range(TOK):
                    ins = dve.tensor_scalar(diag[:, tok, :], ident[:], rstd[:, tok:tok + 1], None, ALU.mult)
                ins.then_inc(s["diag_done"], 1)
                for u in range(6, 14):
                    lo(b + u)
                if kind == "fox":
                    dve.wait_ge(s["f_ready"], 1)
                    for tok in range(TOK):
                        ins = dve.scalar_tensor_tensor(fz[:, tok, :], t_bank[0][:, tok * HEADS:(tok + 1) * HEADS],
                                                       rstd[:, tok:tok + 1], bf[:], ALU.mult, ALU.add)
                    ins.then_inc(s["fz_done"], 1)
                    dve.wait_ge(s["fln_done"], 1)
                    dve.scalar_tensor_tensor(logf[:], fz[:], 0.0, fe[:], ALU.min, ALU.subtract)\
                        .then_inc(s["logf_done"], 1)
                dve.wait_ge(s["rbc_done"], at(phase, "rbc_done") + 1)
                q_evac(b + 8, 0, 0)
                lo(b + 14)
                lo(b + 15)
                k_evac(b + 8, 0, 0)
                if kind == "fox":
                    dve.wait_ge(s["c_ready"], 1)
                    dve.tensor_copy(ct[:], t_bank[1][0:HEADS, 0:S]).then_inc(s["ct_done"], 1)
                    dve.tensor_copy(cn[:].rearrange("p a b -> p (a b)"), t_bank[0][:, 0:TOK * HEADS])\
                        .then_inc(s["cn_done"], 1)
                    dve.wait_ge(s["cn_done"], 1)
                first_part(0)
                second_part(0, 0)
                q_evac(b + 12, 0, 1)
                k_evac(b + 12, 0, 1)
                with dve.Fori(0, PAIRS // 2 - 1) as i:
                    cycle(b + 16, i, 2 * i, 0)
                    cycle(b + 20, i, 2 * i + 1, 1)
                cycle(b + 40, 0, PAIRS - 2, 0, False)
                y_part(PAIRS - 1)

            def chunks(phase, evac=None):
                b, n = at(phase, "units"), dict(PHASES)[phase]["units"] // RING

                def body(b, i, m0):
                    for e in range(2):
                        for j in range(4):
                            lo(b + 4 * e + AHEAD + j, i)
                        if evac:
                            evac(m0 + e, e, b + 4 * e + 3, i)
                if n > 1:
                    with dve.Fori(0, n - 1) as i:
                        body(b, i, 2 * i)
                body(b + RING * (n - 1), 0, 2 * (n - 1))

            def gate_bias(m, e, c, i):
                for tok in range(TOK):
                    consumed(dve, c, i)
                    g = gates[:, tok, ds(m * 512, 512)]
                    dve.scalar_tensor_tensor(g, bank[2 * e + tok][:], rstd[:, tok:tok + 1], g,
                                             ALU.mult, ALU.add).then_inc(s["pj_done"], 1)

            def gated(phase, half):
                def evac(m, e, c, i):
                    for tok in range(TOK):
                        consumed(dve, c, i)
                        g = gates[:, tok, half * D + m * 512:half * D + (m + 1) * 512]
                        v = side[:, tok, m * 512:(m + 1) * 512]
                        if half:
                            dve.tensor_tensor(v, bank[2 * e + tok][:], g, ALU.mult).then_inc(s["pj_done"], 1)
                        else:
                            t = work[1][:, tok, :]
                            dve.tensor_tensor(t, bank[2 * e + tok][:], g, ALU.mult).then_inc(s["pj_done"], 1)
                            dve.wait_ge(s["pj_done"], at(phase, "pj_done") + 2 * m + tok + 1)
                            dve.tensor_tensor(v, v, t, ALU.add).then_inc(s["m_done"], 1)
                return evac

            def w_o(phase, between):
                b = at(phase, "units")
                for u in range(4, 8):
                    lo(b + u)
                add_half(phase, 1.0, 0, b + 3)
                for u in (8, 9):
                    lo(b + u)
                between()
                for u in (10, 11):
                    lo(b + u)
                add_half(phase, 1.0, 1, b + 7)

            dve.sem_inc(s["lo_ready"], RING)
            dve.wait_ge(s["gain_ready"], 1)
            dve.tensor_copy(gain[:, 0:8], bank[0][:, 0:8]).then_inc(s["gain_cols"], 1)
            dve.wait_ge(s["gain_cols"], 1)
            turned("turn_ff1", 0, [(xt_lo, xt_hi, 0)])
            lo(0)
            turned("turn_ff1", 1, [(xt_lo, xt_hi, 0)])
            for u in range(1, AHEAD):
                lo(u)

            def first_stats():
                root("stat_ff1")
                dve.wait_ge(s["gain_ready"], 2)
                dve.tensor_copy(gain[:, 8:76], bank[0][:, 8:76]).then_inc(s["gain_cols"], 1)
                dve.wait_ge(s["ws_ready"], 1)
                w3 = bank[1][:].rearrange("p (g t) -> p g t", g=GROUPS)
                dve.memset(wst[CHUNK:P, :, 0:CHUNK], 0.0)
                dve.tensor_copy(wst[0:CHUNK, :, :], w3[0:CHUNK, :, :])
                dve.tensor_copy(wst[CHUNK:P, :, CHUNK:P], w3[CHUNK:P, :, CHUNK:P]).then_inc(s["wst_done"], 1)
                dve.wait_ge(s["gain_cols"], 2)
                dve.tensor_tensor(gain[:, 80:88], gain[:, 68:76], gain[:, 24:32], ALU.mult).then_inc(s["gain_prod"], 1)

            ffn("ff1", N_FF, FFC, FFC, S, first_stats)
            ffn_end("ff1", 0.5, lambda: turned("turn_mix", 0, [(xt_lo, xt_hi, 1)]))
            attention("stick", "stick", lambda: turned("turn_mix", 1, [(xt_lo, xt_hi, 1)]),
                      lambda: root("stat_mix"))
            chunks("a_in")
            for n in range(TOK * GROUPS):
                tok, g = divmod(n, GROUPS)
                dve.wait_ge(s["pj_done"], at("a_in", "pj_done") + 4)
                dve.bn_stats(bn6[:, n, :], a_uv[:, tok, g * GD:(g + 1) * GD]).then_inc(s["bn_done"], 1)
            for n in range(TOK * GROUPS):
                dve.wait_ge(s["bn_done"], n + 1)
                dve.bn_aggr(bn2[:, n, :], bn6[:, n, :]).then_inc(s["bna_done"], 1)
            dve.wait_ge(s["lns_done"], 1)
            dve.reciprocal(ln_rstd[:], ln_rstd[:]).then_inc(s["lnr_done"], 1)
            dve.wait_ge(s["lnr_done"], 1)
            for n in range(TOK * GROUPS):
                tok, g = divmod(n, GROUPS)
                v = a_uv[:, tok, g * GD:(g + 1) * GD]
                dve.tensor_scalar(v, v, bn2[:, n, 0:1], ln_rstd[:, n:n + 1], ALU.subtract, ALU.mult)\
                    .then_inc(s["ln_done2"], 1)
            dve.wait_ge(s["gate_in"], 32)
            chunks("gates", gate_bias)
            for n in range(TOK * GROUPS):
                tok, g = divmod(n, GROUPS)
                if g % 2 == 0:
                    dve.wait_ge(s["smix_ready"], n // 2 + 1)
                u = a_uv[:, tok, D + g * GD:D + (g + 1) * GD]
                dve.scalar_tensor_tensor(u, bank[4 + 2 * tok + g // 2][:, (g % 2) * GD:(g % 2 + 1) * GD],
                                         gain[:, 64 + g:65 + g], u, ALU.add, ALU.mult).then_inc(s["ya_done"], 1)
            dve.wait_ge(s["gate_done"], 8)
            b = at("branch_b", "units")
            evac_b = gated("branch_b", 1)
            for u in range(4, 8):
                lo(b + u)
            evac_b(0, 0, b + 3, 0)
            turned("turn_a", 0, [(xt_lo, xt_hi, None)])
            turned("turn_a", 1, [(xt_lo, xt_hi, None)])
            for u in range(8, 12):
                lo(b + u)
            evac_b(1, 1, b + 7, 0)
            dve.wait_ge(s["pj_done"], at("branch_a", "pj_done"))
            b = at("branch_a", "units")
            evac_a = gated("branch_a", 0)
            for u in range(4, 8):
                lo(b + u)
            evac_a(0, 0, b + 3, 0)
            for u in (8, 9):
                lo(b + u)
            turned("turn_m", 0, [(yt_lo, yt_hi, None)])
            for u in (10, 11):
                lo(b + u)
            evac_a(1, 1, b + 7, 0)
            b = at("w_out", "units")
            lo(b + 4)
            turned("turn_m", 1, [(yt_lo, yt_hi, None)])
            for u in (5, 6, 7):
                lo(b + u)
            add_half("w_out", 1.0, 0, b + 3)
            for u in (8, 9):
                lo(b + u)
            turned("turn_ff2", 0, [(xt_lo, xt_hi, 2)])
            for u in (10, 11):
                lo(b + u)
            add_half("w_out", 1.0, 1, b + 7)
            turned("turn_ff2", 1, [(xt_lo, xt_hi, 2)])
            ffn("ff2", N_FF, FFC, FFC, S, lambda: root("stat_ff2"))
            ffn_end("ff2", 0.5, lambda: turned("turn_moba", 0, [(xt_lo, xt_hi, 10)]))

            def two_roots():
                dve.wait_ge(s["gain_in2"], 16)
                final("stat_final1")
                root("stat_moba")
                dve.wait_ge(s["rstd_done"], at("moba", "rstd_done"))
                dve.tensor_tensor(rstd[:], rstd[:], rstd_f[:], ALU.mult).then_inc(s["rprod_done"], 1)

            dve.wait_ge(s["const2_done"], 8 + HEADS)
            attention("moba", "moba", lambda: turned("turn_moba", 1, [(xt_lo, xt_hi, 10)]), two_roots)
            w_o("w_o0", lambda: turned("turn_mlp0", 0, [(xt_lo, xt_hi, 5)]))
            turned("turn_mlp0", 1, [(xt_lo, xt_hi, 5)])
            ffn("mlp0", N_MLP, MLPC, 0, 2 * S, lambda: root("stat_mlp0"))
            fox_sets = [(xt_lo, xt_hi, 7), (xq_lo, xq_hi, 4)]
            ffn_end("mlp0", 1.0, lambda: turned("turn_fox", 0, fox_sets))
            dve.wait_ge(s["wf_hi_done"], 1)
            dve.tensor_tensor(wf_lo[:], wf[:], wf_hi[:].bitcast(F32), ALU.subtract).then_inc(s["wf_lo_done"], 1)
            attention("fox", "fox", lambda: turned("turn_fox", 1, fox_sets), lambda: root("stat_fox"))
            w_o("w_o1", lambda: turned("turn_mlp1", 0, [(xt_lo, xt_hi, 6)]))
            turned("turn_mlp1", 1, [(xt_lo, xt_hi, 6)])
            ffn("mlp1", N_MLP, MLPC, 0, 2 * S, lambda: root("stat_mlp1"))
            ffn_end("mlp1", 1.0, lambda: None)
            dve.wait_ge(s["row2_in"], 16)
            final("final2")

        @block.tensor
        def _(pe):
            def ready(c, i=0):
                pe.wait_ge(s["lo_ready"], RING + c + 1 + RING * i)

            def three(dst, a, b, first, last):
                for n, (p, q) in enumerate(((a[1], b[0]), (a[0], b[0]), (a[0], b[1]))):
                    ins = pe.matmul(dst, p, q, start=first and n == 0, stop=last and n == 2)
                return ins

            def slot(c, k, w):
                return [buf[:, c % RING, 0:w].rearrange("p (k n) -> p k n", k=k) for buf in (w_hi, w_lo)]

            def part(pairs, k, cols):
                return [buf[:, k, cols] for buf in pairs]

            def tok_cols(tok):
                return slice(tok * P, (tok + 1) * P)

            def turn(phase, src, half, sets=1, wait=None):
                if half:
                    pe.wait_ge(s["tr_lo"], at(phase, "tr_lo") + 4 * sets)
                wait(half)
                for b in range(2):
                    for k in range(4 * half + 2 * b, 4 * half + 2 * b + 2):
                        for tok in range(TOK):
                            o = (k % 2) * S + tok * P
                            ins = pe.transpose(t_bank[b][:, o:o + P], src[:, tok, k * P:(k + 1) * P], ident[:])
                    ins.then_inc(s["tr_ready"], 1)

            def turn_x(phase, half, before, sets=1):
                turn(phase, x, half, sets,
                     lambda half: pe.wait_ge(s["x_done"], at(before, "x_done") + 2 * half + 2))

            def rows_times(c, i, banks, src, js=range(4), first_wait=None, hooks={}):
                for j in js:
                    if j in hooks:
                        hooks[j]()
                    ready(c + j, i)
                    if first_wait:
                        first_wait(j)
                    w = slot(c + j, 2, 1024)
                    for k in (2 * j, 2 * j + 1):
                        for tok in range(TOK):
                            ins = three(banks[tok][:], part(src, k, tok_cols(tok)), [v[:, k % 2, :] for v in w],
                                        k == 0, k == KT - 1)
                    ins.then_inc(s["used"], 1)

            def stationary(phase, sets=1):
                return lambda j: pe.wait_ge(s["tr_lo"], at(phase, "tr_lo") + sets * (2 * j + 2))

            def ffn(phase, turn_phase, n, width, start, end, third=lambda: None, opening=lambda: None):
                b = at(phase, "units")
                tiles_in = width // P

                def up_half(c, i, js, first_wait=None, hooks={}):
                    rows_times(c, i, gu_bank, (xt_hi, xt_lo), js, first_wait, hooks)

                def turn_chunk(m):
                    pe.wait_ge(s["h_done"], at(phase, "h_done") + 2 * m + 2)
                    for t in range(2):
                        for q in range(tiles_in // 2):
                            for tok in range(TOK):
                                o = q * S + tok * P
                                k = t * (tiles_in // 2) + q
                                ins = pe.transpose(t_bank[t][:, o:o + P], work[1][:, tok, k * P:(k + 1) * P],
                                                   ident[:])
                        ins.then_inc(s["ht_ready"], 1)

                def down(c, i, m, last):
                    for j in range(4):
                        if last and j == 3:
                            end()
                        ready(c + j, i)
                        if j == 0:
                            pe.wait_ge(s["ht_lo"], at(phase, "ht_lo") + 2 * m + 2)
                        half, n_k = j // 2, tiles_in // 2
                        w = slot(c + j, n_k, n_k * 512)
                        for k in range(n_k):
                            row = (j % 2) * n_k + k
                            for tok in range(TOK):
                                ins = three(bank[2 * half + tok][:], part((ht_hi, ht_lo), row, tok_cols(tok)),
                                            [v[:, k, :] for v in w], False, last and row == tiles_in - 1)
                        ins.then_inc(s["used"], 1)

                up_half(b, 0, range(4), stationary(turn_phase), {1: start, 2: third})
                opening()
                for q in range(4):
                    pe.matmul(bank[q][:], zeros[:, 0:P], zeros[:], start=True, stop=False)
                with pe.Fori(0, n - 1) as i:
                    pe.wait_ge(s["h_done"], at(phase, "h_done") + 2 * i + 2)
                    up_half(b + 4, i, (0, 1))
                    turn_chunk(i)
                    up_half(b + 4, i, (2, 3))
                    down(b + 8, i, i, False)
                turn_chunk(n - 1)
                down(b + RING * n - 4, 0, n - 1, True)

            def attention(phase, kind, turn_phase, turn_b, fill):
                b = at(phase, "units")
                hp = at(phase, "z_ready")
                sets = 2 if kind == "fox" else 1
                xq = (xq_hi, xq_lo) if kind == "fox" else (xt_hi, xt_lo)
                xkv = (xt_hi, xt_lo)

                def z_bank(e, h):
                    return bank[4 + 2 * e + h] if kind == "stick" else bank[4 + h]

                def project(c, i, n):
                    ready(c + n, i)
                    dst, src = ((q_bank, xq), (k_bank, xkv))[n // 2]
                    w = slot(c + n, 4, 512)
                    for k in range(4 * (n % 2), 4 * (n % 2) + 4):
                        ins = three(dst[:, 0:S], [v[:, k % 4, :] for v in w], part(src, k, slice(0, S)),
                                    k == 0, k == KT - 1)
                    ins.then_inc(s["used"], 1)

                def scores(pr, e):
                    pe.wait_ge(s["qt_done"], at(phase, "qt_done") + pr + 1)
                    pe.wait_ge(s["kt_done"], at(phase, "kt_done") + pr + 1)
                    for h in range(2):
                        rows = slice(h * DH, (h + 1) * DH)
                        q, k, z = qt[rows, e, :], kt[rows, e, :], z_bank(e, h)
                        if kind == "stick":
                            pe.matmul(z[:, 0:S], k[:, 0:P], q[:, 0:S], start=True, stop=True)
                            ins = pe.matmul(z[:, S:3 * P], k[:, P:S], q[:, P:S], start=False, stop=True,
                                            skip_group_check=True)
                        else:
                            pe.matmul(z[:, 0:P], q[:, 0:P], k[:, 0:P], start=True, stop=True)
                            ins = pe.matmul(z[:, P:3 * P], q[:, P:S], k[:, 0:S], start=False,
                                            stop=True, skip_group_check=True)
                            if kind == "fox":
                                c = c_row[0:1, ds((2 * pr + h) * S, S)]
                                pe.matmul(z[:, 0:P], nones[0:1, :], c_row[0:1, ds((2 * pr + h) * S, P)],
                                          start=False, stop=True, skip_group_check=True)
                                ins = pe.matmul(z[:, P:3 * P], nones[0:1, :], c, start=False, stop=True,
                                                skip_group_check=True)
                        ins.then_inc(s["z_ready"], 1)

                def middle(pr, e):
                    for h in range(2):
                        if kind == "stick":
                            pe.wait_ge(s["spm_done"], at(phase, "spm_done") + 2 * pr + h + 1)
                            z, sp = z_bank(e, h), work[1]
                            pe.matmul(z[:, 0:S], ntri[:], sp[:, h, 0:S], start=False, stop=True,
                                      skip_group_check=True)
                            pe.matmul(z[:, P:S], nones[:], sp[:, h, S:3 * P], start=False, stop=True,
                                      skip_group_check=True)
                            ins = pe.matmul(z[:, S:3 * P], ntri[:], sp[:, h, S:3 * P], start=False, stop=True,
                                            skip_group_check=True)
                        else:
                            pe.wait_ge(s["pn_done"], at(phase, "pn_done") + 2 * pr + h + 1)
                            for o in range(3):
                                ins = pe.transpose(t_bank[h][:, o * P:(o + 1) * P],
                                                   work[1][:, h, o * P:(o + 1) * P], ident[:])
                        ins.then_inc(s["r_ready"], 1)

                def weighted(pr, e):
                    pe.wait_ge(s["v_done"], at(phase, "v_done") + pr + 1)
                    for h in range(2):
                        if kind == "stick":
                            pe.wait_ge(s["wm_done"], at(phase, "wm_done") + 2 * pr + h + 1)
                        else:
                            pe.wait_ge(s["w_done"], hp + 2 * pr + h + 1)
                        rows, cols = slice(h * DH, (h + 1) * DH), slice(h * DH, (h + 1) * DH)
                        pe.matmul(y_bank[rows, 0:S], vn[:, e, 0, cols], work[2][:, h, 0:S],
                                  start=True, stop=False)
                        ins = pe.matmul(y_bank[rows, P:S], vn[:, e, 1, cols], work[2][:, h, S:3 * P],
                                        start=False, stop=True)
                    ins.then_inc(s["y_ready"], 1)

                def cycle(c, i, pr, e):
                    middle(pr, e)
                    scores(pr + 1, 1 - e)
                    project(c, i, 0)
                    weighted(pr, e)
                    for n in (1, 2, 3):
                        project(c, i, n)

                rows_times(b, 0, bank[0:2], xkv, first_wait=stationary(turn_phase, sets), hooks={1: turn_b})
                rows_times(b + 4, 0, bank[2:4], xkv)
                if kind == "fox":
                    pe.wait_ge(s["wf_lo_done"], 1)
                    for tok in range(TOK):
                        for k in range(KT):
                            ins = three(t_bank[0][:, tok * HEADS:(tok + 1) * HEADS],
                                        part(xkv, k, tok_cols(tok)), [v[:, k, :] for v in (wf_hi, wf_lo)],
                                        k == 0, k == KT - 1)
                    ins.then_inc(s["f_ready"], 1)
                pe.wait_ge(s["diag_done"], at(phase, "diag_done") + 1)
                for tok in range(TOK):
                    ins = pe.matmul(rbc_bank[:, tok * P:(tok + 1) * P], ones[:], diag[:, tok, :],
                                    start=True, stop=True)
                ins.then_inc(s["rbc_ready"], 1)
                pe.wait_ge(s["vall_done"], at(phase, "vall_done") + 2)
                for n in range(4):
                    project(b + 8, 0, n)
                if kind == "fox":
                    pe.wait_ge(s["logf_done"], 1)
                    l0, l1, ctp, cnp = logf[:, 0, :], logf[:, 1, :], t_bank[1], t_bank[0]
                    pe.matmul(ctp[0:HEADS, 0:P], l0, tri[:], start=True, stop=True)
                    pe.matmul(ctp[0:HEADS, P:S], l0, ones[:], start=True, stop=False)
                    pe.matmul(ctp[0:HEADS, P:S], l1, tri[:], start=False, stop=True)
                    pe.matmul(cnp[:, 0:HEADS], tri[:], l0, start=True, stop=True)
                    pe.matmul(cnp[:, HEADS:2 * HEADS], ones[:], l0, start=True, stop=False)
                    pe.matmul(cnp[:, HEADS:2 * HEADS], tri[:], l1, start=False, stop=True)\
                        .then_inc(s["c_ready"], 1)
                if kind == "fox":
                    pe.wait_ge(s["qt_done"], at(phase, "qt_done") + 1)
                    pe.wait_ge(s["kt_done"], at(phase, "kt_done") + 1)
                    for n in range(4):
                        project(b + 12, 0, n)
                    pe.wait_ge(s["cn_done"], 1)
                    pe.wait_ge(s["c_row_in"], 16)
                    scores(0, 0)
                else:
                    scores(0, 0)
                    for n in range(4):
                        project(b + 12, 0, n)
                pe.wait_ge(s["vall_done"], at(phase, "vall_done") + 4)
                with pe.Fori(0, PAIRS // 2 - 1) as i:
                    cycle(b + 16, i, 2 * i, 0)
                    cycle(b + 20, i, 2 * i + 1, 1)
                middle(PAIRS - 2, 0)
                scores(PAIRS - 1, 1)
                weighted(PAIRS - 2, 0)
                early = 2 if kind == "stick" else 3
                for j in range(early):
                    fill(j)
                middle(PAIRS - 1, 1)
                for j in range(early, 3):
                    fill(j)
                pe.wait_ge(s["y_lo"], at(phase, "y_lo") + PAIRS - 1)
                weighted(PAIRS - 1, 1)
                fill(3)

            def chunk(phase, c, i, m, e, src, first_wait=None, hooks={}, bank_wait=False):
                if bank_wait:
                    pe.wait_ge(s["pj_done"], at(phase, "pj_done") + 2 * m - 2)
                rows_times(c, i, bank[2 * e:2 * e + 2], src, first_wait=first_wait, hooks=hooks)

            def fill_with(phase, src, first_wait=None):
                return lambda j: rows_times(at(phase, "units"), 0, bank[0:2], src, (j,), first_wait)

            def outputs(phase):
                return lambda j: pe.wait_ge(s["y_lo"], at(phase, "y_lo") + 2 * j + 2)

            XT, YT = (xt_hi, xt_lo), (yt_hi, yt_lo)

            pe.sem_inc(s["used"], RING)
            pe.wait_ge(s["zero_done"], 2)
            pe.wait_ge(s["const_done"], 6)
            pe.wait_ge(s["gain_in"], 16)
            pe.transpose(bank[0][:, 0:8], gain_rows[0:8, :], ident[0:8, 0:8]).then_inc(s["gain_ready"], 1)

            def x_loaded(half):
                pe.wait_ge(s["x_in"], 32)

            turn("turn_ff1", x, 0, 1, x_loaded)
            turn("turn_ff1", x, 1, 1, x_loaded)

            def small_turns():
                pe.wait_ge(s["gain_cols"], 1)
                pe.wait_ge(s["rows_in"], 16 * 9)
                pe.transpose(bank[0][:, 0:76], gain_rows[0:76, :], ident[0:76, 0:76]).then_inc(s["gain_ready"], 1)
                pe.wait_ge(s["ws_in"], 16)
                for g in range(GROUPS):
                    ins = pe.transpose(bank[1][:, g * P:(g + 1) * P], ws[:, g, :], ident[:])
                ins.then_inc(s["ws_ready"], 1)

            def small_taken():
                pe.wait_ge(s["gain_cols"], 2)
                pe.wait_ge(s["wst_done"], 1)

            ffn("ff1", "turn_ff1", N_FF, FFC, lambda: None, lambda: turn_x("turn_mix", 0, "ff1"),
                small_turns, small_taken)
            attention("stick", "stick", "turn_mix", lambda: turn_x("turn_mix", 1, "ff1"), fill_with("a_in", XT))
            pe.wait_ge(s["y_lo"], PAIRS)
            b = at("a_in", "units")
            chunk("a_in", b + 4, 0, 1, 1, XT)
            with pe.Fori(1, 2) as i:
                for e in range(2):
                    chunk("a_in", b + 4 * e, i, 2 * i + e, e, XT, bank_wait=True)
            b = at("gates", "units")
            with pe.Fori(0, 2) as i:
                for e in range(2):
                    chunk("gates", b + 4 * e, i, 2 * i + e, e, XT, bank_wait=True)
            for n in range(TOK * GROUPS):
                tok, g = divmod(n, GROUPS)
                pe.wait_ge(s["v_ln"], tok + 1)
                ins = pe.matmul(bank[4 + 2 * tok + g // 2][:, (g % 2) * GD:(g % 2 + 1) * GD], wst[:, g, :],
                                a_uv[:, tok, g * GD:(g + 1) * GD], start=True, stop=True)
                if g % 2:
                    ins.then_inc(s["smix_ready"], 1)
            u_half = a_uv[:, :, D:2 * D]

            def ya_written(half):
                pe.wait_ge(s["ya_done"], TOK * GROUPS)

            pe.wait_ge(s["pj_done"], at("branch_b", "pj_done"))
            b = at("branch_b", "units")
            chunk("branch_b", b, 0, 0, 0, YT)
            turn("turn_a", u_half, 0, 1, ya_written)
            chunk("branch_b", b + 4, 0, 1, 1, YT, hooks={1: lambda: turn("turn_a", u_half, 1, 1, ya_written)})
            b = at("branch_a", "units")
            pe.wait_ge(s["pj_done"], at("branch_a", "pj_done") - 2)
            chunk("branch_a", b, 0, 0, 0, XT, stationary("turn_a"))
            pe.wait_ge(s["pj_done"], at("branch_a", "pj_done"))

            def turn_m(half):
                turn("turn_m", side, half, 1, lambda half: pe.wait_ge(s["m_done"], 2 * half + 2))

            chunk("branch_a", b + 4, 0, 1, 1, XT, hooks={3: lambda: turn_m(0)})
            b = at("w_out", "units")
            chunk("w_out", b, 0, 0, 0, YT, stationary("turn_m"), {1: lambda: turn_m(1)})
            chunk("w_out", b + 4, 0, 1, 1, YT, hooks={3: lambda: turn_x("turn_ff2", 0, "w_out")})
            ffn("ff2", "turn_ff2", N_FF, FFC, lambda: turn_x("turn_ff2", 1, "w_out"),
                lambda: turn_x("turn_moba", 0, "ff2"))
            attention("moba", "moba", "turn_moba", lambda: turn_x("turn_moba", 1, "ff2"),
                      fill_with("w_o0", YT, outputs("moba")))
            chunk("w_o0", at("w_o0", "units") + 4, 0, 1, 1, YT, hooks={3: lambda: turn_x("turn_mlp0", 0, "w_o0")})
            ffn("mlp0", "turn_mlp0", N_MLP, MLPC, lambda: turn_x("turn_mlp0", 1, "w_o0"),
                lambda: turn_x("turn_fox", 0, "mlp0", 2))
            attention("fox", "fox", "turn_fox", lambda: turn_x("turn_fox", 1, "mlp0", 2),
                      fill_with("w_o1", YT, outputs("fox")))
            chunk("w_o1", at("w_o1", "units") + 4, 0, 1, 1, YT, hooks={3: lambda: turn_x("turn_mlp1", 0, "w_o1")})
            ffn("mlp1", "turn_mlp1", N_MLP, MLPC, lambda: turn_x("turn_mlp1", 1, "w_o1"), lambda: None)


_INS = ["x", "ff1_norm", "ff1_w_gate", "ff1_w_up", "ff1_w_down", "mix_norm", "w_in", "b_gate", "gmlp_ln_g",
        "gmlp_ln_b", "gmlp_w_s", "gmlp_b_s", "w_branch_a", "w_branch_b", "w_out", "ff2_norm", "ff2_w_gate",
        "ff2_w_up", "ff2_w_down", "final_norm", "attn_norm_2", "moba_w_qkv_2", "fox_w_q_2", "w_o_2", "kv_norm_2",
        "w_kv_2", "w_f_2", "b_f_2", "mlp_norm_2", "w_up_2", "w_down_2", "final_norm_2"]


def kernel(**inputs):
    import concourse.bacc as _bacc
    from concourse.bass_utils import run_bass_kernel_spmd as _run

    nc = _bacc.Bacc("TRN2", target_bir_lowering=False, num_devices=1)
    arrays, args = {}, []
    for name in _INS:
        a = np.ascontiguousarray(inputs[name])
        arrays[f"in_{name}"] = a
        args.append(nc.dram_tensor(f"in_{name}", a.shape, mybir.dt.from_np(a.dtype), kind="ExternalInput").ap())
    args.append(nc.dram_tensor("out_x", (1, S, D), F32, kind="ExternalOutput").ap())
    two_blocks(nc, *args)
    return _run(nc, [arrays], core_ids=[0]).results[0]["out_x"]
```
